# Optimizing a Trainium2 kernel written in Bass

```python
import jax, jax.numpy as jnp
from jax import lax
import numpy as np
import math

D_MODEL = 1024
BATCH = 1
SEQ = 256
DEPTH = 2

HEAD_DIM = 64
NSA_HEADS = 8
NSA_KV_HEADS = 2
NSA_GROUP = NSA_HEADS // NSA_KV_HEADS
MOBA_HEADS = 8
MIX_WIDTH = (NSA_HEADS + MOBA_HEADS) * HEAD_DIM
ROT_DIM = HEAD_DIM // 4
ROPE_THETA = 500000.0
CMP_LEN = 32
CMP_STRIDE = 16
CMP_HIDDEN = 256
SLC_BLOCK = 64
SLC_TOPN = 16
WINDOW = 512
MOBA_BLOCK = 256
MOBA_TOPK = 3
Q_BLOCK = 128
SLC_CHUNK = 128
MOBA_CHUNK = 32
D_FF = 2816
EPS = 1e-6
NEG = -1e30
FORCE_BONUS = 1e4

NSA_Q_COLS = NSA_HEADS * HEAD_DIM
NSA_KV_COLS = 3 * 2 * NSA_KV_HEADS * HEAD_DIM
NSA_GATE_COLS = NSA_HEADS * 3
MOBA_COLS = 3 * MOBA_HEADS * HEAD_DIM
IN_COLS = NSA_Q_COLS + NSA_KV_COLS + NSA_GATE_COLS + MOBA_COLS


def rms_norm(x, g):
    xf = x.astype(jnp.float32)
    y = xf * lax.rsqrt(jnp.mean(xf * xf, axis=-1, keepdims=True) + EPS)
    return (y * g.astype(jnp.float32)).astype(x.dtype)

def swiglu(x, w_gate, w_up, w_down):
    return (jax.nn.silu(x @ w_gate) * (x @ w_up)) @ w_down

def rope_tables(S):
    inv_freq = jnp.power(ROPE_THETA, -(jnp.arange(0, ROT_DIM, 2, dtype=jnp.float32) / ROT_DIM))
    ang = jnp.arange(S, dtype=jnp.float32)[:, None] * inv_freq[None, :]
    return jnp.cos(ang), jnp.sin(ang)

def apply_partial_rope(x, cos, sin):
    half = ROT_DIM // 2
    cos = cos.astype(x.dtype)
    sin = sin.astype(x.dtype)
    x1 = x[..., :half]
    x2 = x[..., half:ROT_DIM]
    return jnp.concatenate([x1 * cos - x2 * sin, x2 * cos + x1 * sin, x[..., ROT_DIM:]], axis=-1)

def masked_softmax(s, valid):
    s = jnp.where(valid, s.astype(jnp.float32), NEG)
    m = jnp.max(s, axis=-1, keepdims=True)
    p = jnp.where(valid, jnp.exp(s - m), 0.0)
    return p / jnp.maximum(jnp.sum(p, axis=-1, keepdims=True), 1.0)

def nsa_mixer(q, k_cmp, v_cmp, k_slc, v_slc, k_win, v_win, gates,
              pos_ck, w_ck1, w_ck2, pos_cv, w_cv1, w_cv2, cos, sin):
    B, G, R, S, Dh = q.shape
    scale = Dh ** -0.5
    t = jnp.arange(S)
    q_rot = apply_partial_rope(q, cos, sin)
    k_slc = apply_partial_rope(k_slc, cos, sin)
    k_win = apply_partial_rope(k_win, cos, sin)

    n_cmp = (S - CMP_LEN) // CMP_STRIDE + 1
    starts = jnp.arange(n_cmp) * CMP_STRIDE
    cidx = starts[:, None] + jnp.arange(CMP_LEN)[None, :]

    def compress(k, pos, w1, w2):
        blocks = k[:, :, cidx, :] + pos
        flat = blocks.reshape(B, G, n_cmp, CMP_LEN * Dh)
        return jax.nn.gelu(flat @ w1) @ w2

    kc = compress(k_cmp, pos_ck, w_ck1, w_ck2)
    vc = compress(v_cmp, pos_cv, w_cv1, w_cv2)
    s_c = jnp.einsum('bgrqd,bgnd->bgrqn', q, kc) * scale
    valid_c = (starts + CMP_LEN - 1)[None, :] <= t[:, None]
    p_c = masked_softmax(s_c, valid_c)
    o_cmp = jnp.einsum('bgrqn,bgnd->bgrqd', p_c.astype(vc.dtype), vc)

    n_slc = S // SLC_BLOCK
    top_n = min(SLC_TOPN, n_slc)
    sb = jnp.arange(n_slc) * SLC_BLOCK
    overlap = ((starts[:, None] < (sb + SLC_BLOCK)[None, :]) &
               ((starts + CMP_LEN)[:, None] > sb[None, :])).astype(jnp.float32)
    imp = jnp.einsum('bgrqn,nj->bgqj', p_c, overlap)
    qblk = t // SLC_BLOCK
    j = jnp.arange(n_slc)
    forced = (j[None, :] == 0) | (j[None, :] == qblk[:, None]) | (j[None, :] == qblk[:, None] - 1)
    visible = sb[None, :] <= t[:, None]
    score = jnp.where(visible, jnp.where(forced, FORCE_BONUS, imp), NEG)
    sel_idx = lax.top_k(score, top_n)[1]

    ks_blocks = k_slc.reshape(B, G, n_slc, SLC_BLOCK, Dh)
    vs_blocks = v_slc.reshape(B, G, n_slc, SLC_BLOCK, Dh)
    bi = jnp.arange(B)[:, None, None, None]
    gi = jnp.arange(G)[None, :, None, None]

    def slc_chunk(c):
        q0 = c * SLC_CHUNK
        qc = lax.dynamic_slice_in_dim(q_rot, q0, SLC_CHUNK, axis=3)
        ic = lax.dynamic_slice_in_dim(sel_idx, q0, SLC_CHUNK, axis=2)
        kg = ks_blocks[bi, gi, ic]
        vg = vs_blocks[bi, gi, ic]
        s = jnp.einsum('bgrqd,bgqnld->bgrqnl', qc, kg) * scale
        kpos = ic[..., None] * SLC_BLOCK + jnp.arange(SLC_BLOCK)
        tq = q0 + jnp.arange(SLC_CHUNK)
        valid = (kpos <= tq[None, None, :, None, None]).reshape(B, G, 1, SLC_CHUNK, top_n * SLC_BLOCK)
        p = masked_softmax(s.reshape(B, G, R, SLC_CHUNK, top_n * SLC_BLOCK), valid)
        p = p.reshape(B, G, R, SLC_CHUNK, top_n, SLC_BLOCK).astype(vg.dtype)
        return jnp.einsum('bgrqnl,bgqnld->bgrqd', p, vg)

    o_slc = lax.map(slc_chunk, jnp.arange(S // SLC_CHUNK))
    o_slc = jnp.moveaxis(o_slc, 0, 3).reshape(B, G, R, S, Dh)

    n_qb = S // Q_BLOCK
    kw_pad = jnp.pad(k_win, ((0, 0), (0, 0), (WINDOW, 0), (0, 0)))
    vw_pad = jnp.pad(v_win, ((0, 0), (0, 0), (WINDOW, 0), (0, 0)))
    widx = jnp.arange(n_qb)[:, None] * Q_BLOCK + jnp.arange(WINDOW + Q_BLOCK)[None, :]
    kw = kw_pad[:, :, widx]
    vw = vw_pad[:, :, widx]
    qw = q_rot.reshape(B, G, R, n_qb, Q_BLOCK, Dh)
    s_w = jnp.einsum('bgrcqd,bgckd->bgrcqk', qw, kw) * scale
    kpos = widx - WINDOW
    tq = jnp.arange(n_qb)[:, None] * Q_BLOCK + jnp.arange(Q_BLOCK)[None, :]
    diff = tq[:, :, None] - kpos[:, None, :]
    valid_w = (diff >= 0) & (diff < WINDOW) & (kpos[:, None, :] >= 0)
    p_w = masked_softmax(s_w, valid_w).astype(vw.dtype)
    o_win = jnp.einsum('bgrcqk,bgckd->bgrcqd', p_w, vw).reshape(B, G, R, S, Dh)

    g = jax.nn.sigmoid(gates)
    return g[..., 0:1] * o_cmp + g[..., 1:2] * o_slc + g[..., 2:3] * o_win

def moba_mixer(q, k, v, cos, sin):
    B, H, S, Dh = q.shape
    scale = Dh ** -0.5
    q = apply_partial_rope(q, cos, sin)
    k = apply_partial_rope(k, cos, sin)
    n_blk = -(-S // MOBA_BLOCK)
    pad = n_blk * MOBA_BLOCK - S
    kb = jnp.pad(k, ((0, 0), (0, 0), (0, pad), (0, 0))).reshape(B, H, n_blk, MOBA_BLOCK, Dh)
    vb = jnp.pad(v, ((0, 0), (0, 0), (0, pad), (0, 0))).reshape(B, H, n_blk, MOBA_BLOCK, Dh)
    k_mean = jnp.mean(kb.astype(jnp.float32), axis=3)
    t = jnp.arange(S)
    qblk = t // MOBA_BLOCK
    past = jnp.arange(n_blk)[None, :] < qblk[:, None]
    gate = jnp.einsum('bhqd,bhnd->bhqn', q.astype(jnp.float32), k_mean)
    gate = jnp.where(past, gate, NEG)
    kk = max(min(MOBA_TOPK, n_blk - 1), 1)
    idx = lax.top_k(gate, kk)[1]
    sel_valid = idx < qblk[None, None, :, None]
    bi = jnp.arange(B)[:, None, None, None]
    hi = jnp.arange(H)[None, :, None, None]

    def chunk(c):
        q0 = c * MOBA_CHUNK
        qc = lax.dynamic_slice_in_dim(q, q0, MOBA_CHUNK, axis=2)
        ic = lax.dynamic_slice_in_dim(idx, q0, MOBA_CHUNK, axis=2)
        vc_ = lax.dynamic_slice_in_dim(sel_valid, q0, MOBA_CHUNK, axis=2)
        kg = kb[bi, hi, ic]
        vg = vb[bi, hi, ic]
        s_past = jnp.einsum('bhqd,bhqnld->bhqnl', qc, kg).reshape(B, H, MOBA_CHUNK, kk * MOBA_BLOCK)
        own = q0 // MOBA_BLOCK
        ko = lax.dynamic_index_in_dim(kb, own, axis=2, keepdims=False)
        vo = lax.dynamic_index_in_dim(vb, own, axis=2, keepdims=False)
        s_own = jnp.einsum('bhqd,bhld->bhql', qc, ko)
        tq = q0 + jnp.arange(MOBA_CHUNK)
        own_valid = (own * MOBA_BLOCK + jnp.arange(MOBA_BLOCK))[None, :] <= tq[:, None]
        valid = jnp.concatenate([
            jnp.broadcast_to(vc_[..., None], (B, H, MOBA_CHUNK, kk, MOBA_BLOCK)).reshape(B, H, MOBA_CHUNK, kk * MOBA_BLOCK),
            jnp.broadcast_to(own_valid, (B, H, MOBA_CHUNK, MOBA_BLOCK))], axis=-1)
        s = jnp.concatenate([s_past, s_own], axis=-1) * scale
        p = masked_softmax(s, valid).astype(vg.dtype)
        p_past = p[..., :kk * MOBA_BLOCK].reshape(B, H, MOBA_CHUNK, kk, MOBA_BLOCK)
        p_own = p[..., kk * MOBA_BLOCK:]
        return (jnp.einsum('bhqnl,bhqnld->bhqd', p_past, vg) +
                jnp.einsum('bhql,bhld->bhqd', p_own, vo))

    o = lax.map(chunk, jnp.arange(S // MOBA_CHUNK))
    return jnp.moveaxis(o, 0, 2).reshape(B, H, S, Dh)

def hybrid_mixer(h, w_in, pos_ck, w_ck1, w_ck2, pos_cv, w_cv1, w_cv2, w_out, cos, sin):
    B, S, _ = h.shape
    G, R, Dh = NSA_KV_HEADS, NSA_GROUP, HEAD_DIM
    proj = h @ w_in
    q_n, kv_n, gate_n, moba = jnp.split(
        proj, [NSA_Q_COLS, NSA_Q_COLS + NSA_KV_COLS, NSA_Q_COLS + NSA_KV_COLS + NSA_GATE_COLS], axis=-1)
    q_n = q_n.reshape(B, S, G, R, Dh).transpose(0, 2, 3, 1, 4)
    kv_n = kv_n.reshape(B, S, 6, G, Dh).transpose(2, 0, 3, 1, 4)
    gate_n = gate_n.reshape(B, S, G, R, 3).transpose(0, 2, 3, 1, 4)
    o_nsa = nsa_mixer(q_n, kv_n[0], kv_n[1], kv_n[2], kv_n[3], kv_n[4], kv_n[5], gate_n,
                      pos_ck, w_ck1, w_ck2, pos_cv, w_cv1, w_cv2, cos, sin)
    o_nsa = o_nsa.transpose(0, 3, 1, 2, 4).reshape(B, S, NSA_HEADS * Dh)
    qkv_m = moba.reshape(B, S, 3, MOBA_HEADS, Dh).transpose(2, 0, 3, 1, 4)
    o_moba = moba_mixer(qkv_m[0], qkv_m[1], qkv_m[2], cos, sin)
    o_moba = o_moba.transpose(0, 2, 1, 3).reshape(B, S, MOBA_HEADS * Dh)
    return jnp.concatenate([o_nsa, o_moba], axis=-1) @ w_out

def first_inputs(seed: int = 0) -> dict:
    key = jax.random.key(seed)
    ks = jax.random.split(key, 19)

    def w(k, shape, fan_in):
        return jax.random.normal(k, shape, jnp.float32) * fan_in ** -0.5

    def gain(k, shape):
        return 1.0 + 0.02 * jax.random.normal(k, shape, jnp.float32)

    return {
        "x": jax.random.normal(ks[0], (BATCH, SEQ, D_MODEL), jnp.float32),
        "norm_ffn1": gain(ks[1], (DEPTH, D_MODEL)),
        "w_ffn1_gate": w(ks[2], (DEPTH, D_MODEL, D_FF), D_MODEL),
        "w_ffn1_up": w(ks[3], (DEPTH, D_MODEL, D_FF), D_MODEL),
        "w_ffn1_down": w(ks[4], (DEPTH, D_FF, D_MODEL), D_FF),
        "norm_mix": gain(ks[5], (DEPTH, D_MODEL)),
        "w_in": w(ks[6], (DEPTH, D_MODEL, IN_COLS), D_MODEL),
        "pos_ck": 0.1 * jax.random.normal(ks[7], (DEPTH, CMP_LEN, HEAD_DIM), jnp.float32),
        "w_ck1": w(ks[8], (DEPTH, CMP_LEN * HEAD_DIM, CMP_HIDDEN), CMP_LEN * HEAD_DIM),
        "w_ck2": w(ks[9], (DEPTH, CMP_HIDDEN, HEAD_DIM), CMP_HIDDEN),
        "pos_cv": 0.1 * jax.random.normal(ks[10], (DEPTH, CMP_LEN, HEAD_DIM), jnp.float32),
        "w_cv1": w(ks[11], (DEPTH, CMP_LEN * HEAD_DIM, CMP_HIDDEN), CMP_LEN * HEAD_DIM),
        "w_cv2": w(ks[12], (DEPTH, CMP_HIDDEN, HEAD_DIM), CMP_HIDDEN),
        "w_out": w(ks[13], (DEPTH, MIX_WIDTH, D_MODEL), MIX_WIDTH),
        "norm_ffn2": gain(ks[14], (DEPTH, D_MODEL)),
        "w_ffn2_gate": w(ks[15], (DEPTH, D_MODEL, D_FF), D_MODEL),
        "w_ffn2_up": w(ks[16], (DEPTH, D_MODEL, D_FF), D_MODEL),
        "w_ffn2_down": w(ks[17], (DEPTH, D_FF, D_MODEL), D_FF),
        "norm_final": gain(ks[18], (D_MODEL,)),
    }

def first_block(x, norm_ffn1, w_ffn1_gate, w_ffn1_up, w_ffn1_down, norm_mix, w_in,
              pos_ck, w_ck1, w_ck2, pos_cv, w_cv1, w_cv2, w_out,
              norm_ffn2, w_ffn2_gate, w_ffn2_up, w_ffn2_down, norm_final):
    cos, sin = rope_tables(x.shape[1])
    for l in range(DEPTH):
        x = x + 0.5 * swiglu(rms_norm(x, norm_ffn1[l]), w_ffn1_gate[l], w_ffn1_up[l], w_ffn1_down[l])
        x = x + hybrid_mixer(rms_norm(x, norm_mix[l]), w_in[l], pos_ck[l], w_ck1[l], w_ck2[l],
                             pos_cv[l], w_cv1[l], w_cv2[l], w_out[l], cos, sin)
        x = x + 0.5 * swiglu(rms_norm(x, norm_ffn2[l]), w_ffn2_gate[l], w_ffn2_up[l], w_ffn2_down[l])
    return rms_norm(x, norm_final)


A_HEADS = 8
IDX_HEADS = 4
IDX_DIM = 64
TOPK_MAX = 256
B_HEADS = 4
B_VDIM = 2 * HEAD_DIM
D_A = A_HEADS * HEAD_DIM
D_B = B_HEADS * B_VDIM
FFN_HIDDEN = -(-8 * D_MODEL // (3 * 256)) * 256
ROPE_THETA_2 = 10000.0
DENSE_Q_BLOCK = 128
SPARSE_Q_BLOCK = 32
POS_OFFSET_MAX = 4096
IN_WIDTHS = (D_A, D_A, D_A,
             IDX_HEADS * IDX_DIM, IDX_DIM, IDX_HEADS,
             B_HEADS * 2 * HEAD_DIM, B_HEADS * 2 * HEAD_DIM, D_B,
             2 * D_MODEL)
D_IN = sum(IN_WIDTHS)


def rms_norm_2(x, g):
    x32 = x.astype(jnp.float32)
    y = x32 * lax.rsqrt(jnp.mean(x32 * x32, axis=-1, keepdims=True) + EPS)
    return (y * g.astype(jnp.float32)).astype(x.dtype)

def rope_tables_2(positions):
    inv_freq = 1.0 / (ROPE_THETA_2 ** (jnp.arange(0, HEAD_DIM, 2, dtype=jnp.float32) / HEAD_DIM))
    ang = positions.astype(jnp.float32)[..., None] * inv_freq
    return jnp.cos(ang)[:, :, None, :], jnp.sin(ang)[:, :, None, :]

def apply_rope(x, cos, sin):
    x32 = x.astype(jnp.float32)
    x1, x2 = jnp.split(x32, 2, axis=-1)
    out = jnp.concatenate([x1 * cos - x2 * sin, x2 * cos + x1 * sin], axis=-1)
    return out.astype(x.dtype)

def split_cols(proj):
    offs = np.cumsum(np.array(IN_WIDTHS))[:-1].tolist()
    return jnp.split(proj, offs, axis=-1)

def sparse_attention(q, k, v, q_idx, k_idx, w_idx, k_sel):
    B, S, H, dh = q.shape
    n_blk = S // SPARSE_Q_BLOCK
    key_pos = jnp.arange(S)
    k_idx32 = k_idx.astype(jnp.float32)

    def block(i):
        start = i * SPARSE_Q_BLOCK
        qb = lax.dynamic_slice_in_dim(q, start, SPARSE_Q_BLOCK, axis=1)
        qib = lax.dynamic_slice_in_dim(q_idx, start, SPARSE_Q_BLOCK, axis=1)
        wb = lax.dynamic_slice_in_dim(w_idx, start, SPARSE_Q_BLOCK, axis=1)
        q_pos = start + jnp.arange(SPARSE_Q_BLOCK)
        causal = key_pos[None, :] <= q_pos[:, None]
        dots = jnp.einsum('bqhd,bsd->bqhs', qib.astype(jnp.float32), k_idx32) * (IDX_DIM ** -0.5)
        score = jnp.einsum('bqh,bqhs->bqs', wb.astype(jnp.float32), jax.nn.relu(dots))
        score = jnp.where(causal[None], score, -jnp.inf)
        _, top_idx = lax.top_k(score, k_sel)
        valid = top_idx <= q_pos[None, :, None]
        kg = jax.vmap(lambda kb, ib: kb[ib])(k, top_idx)
        vg = jax.vmap(lambda vb, ib: vb[ib])(v, top_idx)
        logits = jnp.einsum('bqhd,bqkhd->bqhk', qb.astype(jnp.float32),
                            kg.astype(jnp.float32)) * (dh ** -0.5)
        logits = jnp.where(valid[:, :, None, :], logits, -jnp.inf)
        p = jax.nn.softmax(logits, axis=-1).astype(v.dtype)
        return jnp.einsum('bqhk,bqkhd->bqhd', p, vg)

    out = lax.map(block, jnp.arange(n_blk))
    return jnp.moveaxis(out, 0, 1).reshape(B, S, H, dh)

def diff_attention(q, k, v, lam):
    B, S, H, _, dh = q.shape
    n_blk = S // DENSE_Q_BLOCK
    key_pos = jnp.arange(S)
    k32 = k.astype(jnp.float32)

    def block(i):
        start = i * DENSE_Q_BLOCK
        qb = lax.dynamic_slice_in_dim(q, start, DENSE_Q_BLOCK, axis=1)
        q_pos = start + jnp.arange(DENSE_Q_BLOCK)
        causal = key_pos[None, :] <= q_pos[:, None]
        logits = jnp.einsum('bqhcd,bshcd->bhcqs', qb.astype(jnp.float32), k32) * (dh ** -0.5)
        logits = jnp.where(causal[None, None, None], logits, -jnp.inf)
        p = jax.nn.softmax(logits, axis=-1)
        attn = (p[:, :, 0] - lam * p[:, :, 1]).astype(v.dtype)
        return jnp.einsum('bhqs,bshe->bqhe', attn, v)

    out = lax.map(block, jnp.arange(n_blk))
    return jnp.moveaxis(out, 0, 1).reshape(B, S, H, 2 * dh)

def hybrid_layer(x, cos, sin, layer_idx, attn_norm, w_in, gate_bias, a_q_norm, a_k_norm,
                 idx_k_norm, b_q_norm, b_k_norm, diff_lambda, b_subln, w_up_a, w_up_b,
                 w_out, ffn_norm, w_ffn_in, w_ffn_out):
    B, S, _ = x.shape
    k_sel = min(TOPK_MAX, S // 4)
    h = rms_norm_2(x, attn_norm)
    proj = h @ w_in
    aq, ak, av, iq, ik, iw, bq, bk, bv, gates = split_cols(proj)

    aq = apply_rope(rms_norm_2(aq.reshape(B, S, A_HEADS, HEAD_DIM), a_q_norm), cos, sin)
    ak = apply_rope(rms_norm_2(ak.reshape(B, S, A_HEADS, HEAD_DIM), a_k_norm), cos, sin)
    av = av.reshape(B, S, A_HEADS, HEAD_DIM)
    iq = apply_rope(iq.reshape(B, S, IDX_HEADS, IDX_DIM), cos, sin)
    ik = apply_rope(rms_norm_2(ik, idx_k_norm)[:, :, None, :], cos, sin)[:, :, 0, :]
    iw = iw * (IDX_HEADS ** -0.5)
    ya = sparse_attention(aq, ak, av, iq, ik, iw, k_sel).reshape(B, S, D_A)

    bq = apply_rope(rms_norm_2(bq.reshape(B, S, 2 * B_HEADS, HEAD_DIM), b_q_norm), cos, sin)
    bk = apply_rope(rms_norm_2(bk.reshape(B, S, 2 * B_HEADS, HEAD_DIM), b_k_norm), cos, sin)
    bq = bq.reshape(B, S, B_HEADS, 2, HEAD_DIM)
    bk = bk.reshape(B, S, B_HEADS, 2, HEAD_DIM)
    bv = bv.reshape(B, S, B_HEADS, B_VDIM)
    lam_init = 0.8 - 0.6 * math.exp(-0.3 * layer_idx)
    dl = diff_lambda.astype(jnp.float32)
    lam = jnp.exp(jnp.sum(dl[0] * dl[1])) - jnp.exp(jnp.sum(dl[2] * dl[3])) + lam_init
    yb = diff_attention(bq, bk, bv, lam)
    yb = (rms_norm_2(yb, b_subln) * (1.0 - lam_init)).reshape(B, S, D_B)

    g = jax.nn.sigmoid((gates + gate_bias).astype(jnp.float32)).astype(x.dtype)
    g_a, g_b = jnp.split(g, 2, axis=-1)
    merged = g_a * (ya @ w_up_a) + g_b * (yb @ w_up_b)
    x = x + merged @ w_out

    h = rms_norm_2(x, ffn_norm)
    gate, up = jnp.split(h @ w_ffn_in, 2, axis=-1)
    return x + (jax.nn.silu(gate) * up) @ w_ffn_out

def second_inputs(seed: int = 0) -> dict:
    key = jax.random.key(seed)
    ks = jax.random.split(key, 20)
    f32 = jnp.float32

    def dense(k, shape, fan_in):
        return jax.random.normal(k, shape, f32) * (fan_in ** -0.5)

    def gain(k, shape):
        return 1.0 + 0.02 * jax.random.normal(k, shape, f32)

    x = jax.random.normal(ks[0], (BATCH, SEQ, D_MODEL), f32)
    offset = jax.random.randint(ks[1], (BATCH, 1), 0, POS_OFFSET_MAX, dtype=jnp.int32)
    positions = (offset + jnp.arange(SEQ, dtype=jnp.int32)[None, :]).astype(jnp.int32)
    return {
        "x": x,
        "positions": positions,
        "attn_norm": gain(ks[2], (DEPTH, D_MODEL)),
        "w_in": dense(ks[3], (DEPTH, D_MODEL, D_IN), D_MODEL),
        "gate_bias": 0.1 * jax.random.normal(ks[4], (DEPTH, 2 * D_MODEL), f32),
        "a_q_norm": gain(ks[5], (DEPTH, HEAD_DIM)),
        "a_k_norm": gain(ks[6], (DEPTH, HEAD_DIM)),
        "idx_k_norm": gain(ks[7], (DEPTH, IDX_DIM)),
        "b_q_norm": gain(ks[8], (DEPTH, HEAD_DIM)),
        "b_k_norm": gain(ks[9], (DEPTH, HEAD_DIM)),
        "diff_lambda": 0.1 * jax.random.normal(ks[10], (DEPTH, 4, HEAD_DIM), f32),
        "b_subln": gain(ks[11], (DEPTH, B_VDIM)),
        "w_up_a": dense(ks[12], (DEPTH, D_A, D_MODEL), D_A),
        "w_up_b": dense(ks[13], (DEPTH, D_B, D_MODEL), D_B),
        "w_out": dense(ks[14], (DEPTH, D_MODEL, D_MODEL), D_MODEL),
        "ffn_norm": gain(ks[15], (DEPTH, D_MODEL)),
        "w_ffn_in": dense(ks[16], (DEPTH, D_MODEL, 2 * FFN_HIDDEN), D_MODEL),
        "w_ffn_out": dense(ks[17], (DEPTH, FFN_HIDDEN, D_MODEL), FFN_HIDDEN),
    }

def second_block(x, positions, attn_norm, w_in, gate_bias, a_q_norm, a_k_norm, idx_k_norm,
              b_q_norm, b_k_norm, diff_lambda, b_subln, w_up_a, w_up_b, w_out,
              ffn_norm, w_ffn_in, w_ffn_out):
    cos, sin = rope_tables_2(positions)
    for l in range(DEPTH):
        x = hybrid_layer(x, cos, sin, l, attn_norm[l], w_in[l], gate_bias[l], a_q_norm[l],
                         a_k_norm[l], idx_k_norm[l], b_q_norm[l], b_k_norm[l],
                         diff_lambda[l], b_subln[l], w_up_a[l], w_up_b[l], w_out[l],
                         ffn_norm[l], w_ffn_in[l], w_ffn_out[l])
    return x


def setup_inputs(seed=0):
    out = dict(first_inputs(seed))
    for name, value in second_inputs(seed + 1).items():
        if name != "x":
            out[name + "_2"] = value
    return out


def reference(
    x, norm_ffn1, w_ffn1_gate, w_ffn1_up, w_ffn1_down, norm_mix, w_in, pos_ck, w_ck1, w_ck2,
    pos_cv, w_cv1, w_cv2, w_out, norm_ffn2, w_ffn2_gate, w_ffn2_up, w_ffn2_down, norm_final,
    positions_2, attn_norm_2, w_in_2, gate_bias_2, a_q_norm_2, a_k_norm_2, idx_k_norm_2,
    b_q_norm_2, b_k_norm_2, diff_lambda_2, b_subln_2, w_up_a_2, w_up_b_2, w_out_2, ffn_norm_2,
    w_ffn_in_2, w_ffn_out_2,
):
    x = first_block(
        x, norm_ffn1, w_ffn1_gate, w_ffn1_up, w_ffn1_down, norm_mix, w_in, pos_ck, w_ck1, w_ck2,
        pos_cv, w_cv1, w_cv2, w_out, norm_ffn2, w_ffn2_gate, w_ffn2_up, w_ffn2_down, norm_final,
    )
    return second_block(
        x, positions_2, attn_norm_2, w_in_2, gate_bias_2, a_q_norm_2, a_k_norm_2, idx_k_norm_2,
        b_q_norm_2, b_k_norm_2, diff_lambda_2, b_subln_2, w_up_a_2, w_up_b_2, w_out_2,
        ffn_norm_2, w_ffn_in_2, w_ffn_out_2,
    )


_drawn_inputs = setup_inputs


def setup_inputs(seed=0):
    import zlib

    import numpy as np

    out = dict(_drawn_inputs(seed))
    spreads = {}
    factors = {'pos_ck': 4.485,
     'norm_ffn2': 2.704,
     'a_q_norm_2': 8.0,
     'a_k_norm_2': 8.0,
     'idx_k_norm_2': 3.909,
     'b_q_norm_2': 6.398,
     'b_k_norm_2': 6.788,
     'b_subln_2': 3.718,
     'ffn_norm_2': 2.725}
    for name, (base, spread) in spreads.items():
        noise = np.random.default_rng([zlib.crc32(name.encode()), seed]).standard_normal(out[name].shape)
        drawn = base * np.exp(spread * noise) if base else spread * noise
        out[name] = __import__('jax').numpy.asarray(drawn.astype(out[name].dtype))
    for name, factor in factors.items():
        out[name] = (out[name] * factor).astype(out[name].dtype)
    return out
```

```python
import math
from contextlib import ExitStack

import concourse.bass as bass
from concourse import mybir
import numpy as np

ALU = mybir.AluOpType
ACT = mybir.ActivationFunctionType
AX = mybir.AxisListType
F32 = mybir.dt.float32
F32R = mybir.dt.float32r
I32 = mybir.dt.int32

P = 128
SEQ = 256
TT_ = SEQ // P
DM = 1024
KC = DM // P
DFF = 2816
FT = DFF // 256
DH = 64
DEPTH = 2
EPS = 1e-6
NEG = -1e30
TAKEN = -3e38
NCMP = (SEQ - 32) // 16 + 1
SLOTS = 4
UNIT = 2048

WIN1 = [(0, 512), (512, 512), (1024, 280), (1304, 512), (1816, 512), (2328, 512)]
WIN2 = [(0, 512), (512, 512), (1024, 512), (1536, 324), (1860, 512), (2372, 512), (2884, 512)] + \
       [(3396 + 512 * g, 512) for g in range(4)]
IN1 = 2840
IN2 = 5444
GATES2 = 3396

U_UP, U_DOWN, U_OUT = 2 * FT, FT, 4
P1_FFN1 = 0
P1_WIN = P1_FFN1 + U_UP + U_DOWN
P1_CK = P1_WIN + 2 * len(WIN1)
P1_OUT = P1_CK + 4
P1_FFN2 = P1_OUT + U_OUT
U1 = P1_FFN2 + U_UP + U_DOWN
P2_WIN = 0
P2_UPA = P2_WIN + 2 * len(WIN2)
P2_UPB = P2_UPA + 2
P2_OUT = P2_UPB + 2
P2_FFN = P2_OUT + U_OUT
U2 = P2_FFN + U_UP + U_DOWN

JOBS1, JOBS2 = 24, 16
TJ1, TJ2 = 11, 10


def slot_units(u, s):
    return (u - s + SLOTS - 1) // SLOTS


def since_slot(p, before):
    if p >= SLOTS:
        return SLOTS
    return min(min(p + u - q for q in range(u) if q % SLOTS == p % SLOTS) for u in before)


class Stream:

    def __init__(self, l, units, base_units, base_slots, before):
        self.l, self.units, self.base, self.base_slots, self.before = l, units, base_units, base_slots, before

    def index(self, p, it=0):
        return self.l * self.units + it * SLOTS + (self.base + p)

    def loads(self, p, it=0):
        s = p % SLOTS
        return (self.l * slot_units(self.units, s) + it + (self.base_slots[s] + p // SLOTS + 1)) * 32

    def used(self, p, it=0):
        return self.index(p, it) + 1 + SLOTS

    def freed(self, p, it=0):
        return self.index(p, it) + 1 + SLOTS - since_slot(p, self.before)


def stream1(l):
    return Stream(l, U1, 0, [0] * SLOTS, (U1,))


def stream2(l):
    return Stream(l, U2, DEPTH * U1, [DEPTH * slot_units(U1, s) for s in range(SLOTS)], (U1, U2))


def build(nc, I, out):
    L = DEPTH
    with ExitStack() as ctx:
        def sb(name, shape, dt=F32):
            return ctx.enter_context(nc.sbuf_tensor(name, shape, dt))

        def sem(name):
            return ctx.enter_context(nc.semaphore(name))

        raw = sb("raw", [P, SLOTS, UNIT])
        w_hi = sb("w_hi", [P, SLOTS, UNIT], F32R)
        w_lo = sb("w_lo", [P, SLOTS, UNIT], F32R)
        x = sb("x", [P, 2, DM])
        xn = sb("xn", [P, 2, DM])
        aT_hi = sb("aT_hi", [P, KC, SEQ], F32R)
        aT_lo = sb("aT_lo", [P, KC, SEQ], F32R)
        att = sb("att", [P, 2304])
        ident = sb("ident", [P, P])
        causal = sb("causal", [P, 384])
        cmask = sb("cmask", [P, 2, NCMP])
        cvalid = sb("cvalid", [P, 2, NCMP])
        gain_rows = sb("gain_rows", [80, P])
        gain_cols = sb("gain_cols", [P, 80])
        gain_l = sb("gain_l", [P, 3, KC])
        ss = sb("ss", [P, 2])
        rstd = sb("rstd", [P, 2])
        rot1 = sb("rot1", [P, 2, 16])
        neg_max = sb("neg_max", [P, 2, 2])
        sums = sb("sums", [P, 4, 2])
        with ExitStack() as r:
            row_rot = r.enter_context(nc.sbuf_tensor("row_rot", [P, 4, 2, 8, 8], F32))
        with ExitStack() as r:
            score = r.enter_context(nc.sbuf_tensor("score", [P, 384], F32))
        rot_end = sb("rot_end", [P, 512])
        factor = sb("factor", [P, 2])
        with ExitStack() as r:
            gT_hi = r.enter_context(nc.sbuf_tensor("gT_hi", [P, 2 * FT, SEQ], F32R))
            gT_lo = r.enter_context(nc.sbuf_tensor("gT_lo", [P, 2 * FT, SEQ], F32R))
        with ExitStack() as r:
            def rb(name, shape, dt=F32):
                return r.enter_context(nc.sbuf_tensor(name, shape, dt))
            proj1 = rb("proj1", [P, 2, IN1])
            tt1 = rb("tt1", [P, 18, SEQ])
            kflat_hi = rb("kflat_hi", [P, 16 * 30 + 98], F32R)
            kflat_lo = rb("kflat_lo", [P, 16 * 30 + 98], F32R)
            vflat_hi = rb("vflat_hi", [P, 16 * 30 + 98], F32R)
            vflat_lo = rb("vflat_lo", [P, 16 * 30 + 98], F32R)
            pcT = rb("pcT", [16, 8, P])
        with ExitStack() as r:
            proj2 = rb("proj2", [P, 2, IN2])
            tt2 = rb("tt2", [P, 11, SEQ])
        region_end = sb("region_end", [P, 13800])
        with ExitStack() as r:
            pos_rows = r.enter_context(nc.sbuf_tensor("pos_rows", [32, P], F32))
            posT = r.enter_context(nc.sbuf_tensor("posT", [P, 32], F32))
            w_k2 = r.enter_context(nc.sbuf_tensor("w_k2", [P, 2, 2, DH], F32))
            w_v2 = r.enter_context(nc.sbuf_tensor("w_v2", [P, 2, DH], F32))
            h1T = r.enter_context(nc.sbuf_tensor("h1T", [P, 4, 30], F32))
        with ExitStack() as r:
            par2 = r.enter_context(nc.sbuf_tensor("par2", [P, 706], F32))
        par_end = sb("par_end", [P, 720])
        kcT = sb("kcT", [P, 30])
        vc = sb("vc", [16, 2, DH])
        gates1 = sb("gates1", [P, 2, 24])
        cmp_max = sb("cmp_max", [P, 16])
        pos_i = sb("pos_i", [P, 2], I32)
        pos_f = sb("pos_f", [P, 2])
        inv_f = sb("inv_f", [P, 32])
        cs2 = sb("cs2", [P, 2, 2, 32])
        rg = sb("rg", [P, 5, 4, 2, 32])
        row_gain = rg[:, :, :, :, :].rearrange("p a b c d -> p (a b c d)")[:, 0:DM]
        ms = sb("ms", [P, 66])
        lam = sb("lam", [P, 3])
        iw = sb("iw", [P, 2, 4])
        m8 = sb("m8", [P, 2, 8])

        twice1 = tt1[:, 10:14, :].rearrange("p a n -> p (a n)").rearrange("p (i k e d) -> p i k e d", i=2, k=4, e=2)
        twice2 = att[:, 2048:2304].rearrange("p (i e d) -> p i e d", i=2, e=2)
        sil = att[:, 0:1024].rearrange("p (b i n) -> p b i n", b=2, i=2)
        gg = att[:, 1024:2048].rearrange("p (b i n) -> p b i n", b=2, i=2)
        s_sb = att[:, 0:768].rearrange("p (b n) -> p b n", b=2)
        p_sb = att[:, 768:1536].rearrange("p (b n) -> p b n", b=2)
        pT_sb = att[:, 1536:2304].rearrange("p (b n) -> p b n", b=2)
        csc = att[:, 0:240].rearrange("p (i h n) -> p i h n", i=2, h=8)
        cex = att[:, 240:480].rearrange("p (i h n) -> p i h n", i=2, h=8)
        h1 = att[0:30, 480:992].rearrange("p (k n) -> p k n", k=2)
        flat = att[:, 992:992 + 960].rearrange("p (k c g n) -> p k c g n", k=2, c=16, g=2)

        ps = ctx.enter_context(nc.psum_tensor("ps", [P, 8, 512], F32))

        loaded = [sem(f"loaded{s}") for s in range(SLOTS)]
        units_hi = sem("units_hi")
        units_split = sem("units_split")
        units_used = sem("units_used")
        setup_loaded = sem("setup_loaded")
        params1_loaded = sem("params1_loaded")
        params2_loaded = sem("params2_loaded")
        bias_loaded = sem("bias_loaded")
        x_stored = sem("x_stored")
        consts_ready = sem("consts_ready")
        gains_T = sem("gains_T")
        gains_ready = sem("gains_ready")
        x_ready = sem("x_ready")
        squares = sem("squares")
        mean_sq = sem("mean_sq")
        roots = sem("roots")
        xn_ready = sem("xn_ready")
        stage_T = sem("stage_T")
        stage_hi = sem("stage_hi")
        stage_ready = sem("stage_ready")
        silu_done = sem("silu_done")
        g_ready = sem("g_ready")
        g_T = sem("g_T")
        gT_hi_done = sem("gT_hi_done")
        gT_ready = sem("gT_ready")
        down_done = sem("down_done")
        proj_act = sem("proj_act")
        proj_dve = sem("proj_dve")
        pos_T = sem("pos_T")
        pos_ready = sem("pos_ready")
        tj_done = sem("tj_done")
        tj_act = sem("tj_act")
        tj_dve = sem("tj_dve")
        rot_ready = sem("rot_ready")
        twice_ready = sem("twice_ready")
        flat_ready = sem("flat_ready")
        flat_hi_done = sem("flat_hi_done")
        flat_lo_done = sem("flat_lo_done")
        gelu_done = sem("gelu_done")
        h1_T = sem("h1_T")
        h1T_ready = sem("h1T_ready")
        kv_c = sem("kv_c")
        kv_c_ready = sem("kv_c_ready")
        cs_done = sem("cs_done")
        cs_shifted = sem("cs_shifted")
        c_exp = sem("c_exp")
        c_probs = sem("c_probs")
        c_T = sem("c_T")
        cT_ready = sem("cT_ready")
        c_out = sem("c_out")
        c_evac = sem("c_evac")
        gates_done = sem("gates_done")
        scores_done = sem("scores_done")
        scores_masked = sem("scores_masked")
        probs_ready = sem("probs_ready")
        probs_T = sem("probs_T")
        pT_ready = sem("pT_ready")
        attn_done = sem("attn_done")
        attn_evac = sem("attn_evac")
        rope_arg = sem("rope_arg")
        rope_sin = sem("rope_sin")
        lam_sums = sem("lam_sums")
        lam_exp = sem("lam_exp")
        tables_ready = sem("tables_ready")
        par_free = sem("par_free")
        head_sq = sem("head_sq")
        head_sq_used = sem("head_sq_used")
        head_ms = sem("head_ms")
        head_root = sem("head_root")
        idx_done = sem("idx_done")
        idx_relu = sem("idx_relu")
        idx_used = sem("idx_used")
        yb_ms = sem("yb_ms")
        yb_root = sem("yb_root")
        bias_added = sem("bias_added")
        wait_over = sem("wait_over")

        def heads(ap, n):
            return ap.unsqueeze(ap.ndim - 1).broadcast_to(list(ap.shape[:-1]) + [n, ap.shape[-1]])

        def lanes(ap, n):
            return ap.unsqueeze(ap.ndim).broadcast_to(list(ap.shape) + [n])

        def job1(j):
            if j < 8:
                h = j
                return (DH * (h // 4), 4 + h % 4, 8, 512 + 384 - 0 + DH * (h // 4), DH, DH * h, 3 * h + 1)
            if j < 16:
                h = j - 8
                return (DH * (h // 4), 4 + h % 4, 9, 1152 + DH * (h // 4), DH, DH * h, 3 * h + 2)
            h = j - 16
            return (DH * (h % 2), 10 + h // 2, 14 + h // 2, 2328 + DH * h, DH, 512 + DH * h, None)

        def job2(j):
            if j < 8:
                return (DH * (j % 2), j // 2, 4 + j // 2, 1024 + DH * j, DH, DH * j, None)
            h, c = (j - 8) // 2, (j - 8) % 2
            return (DH * c, h, 4 + h, 2884 + P * h, P, 512 + P * h, c)

        def paired(ap):
            return ap.rearrange("p (r g d) -> p g r d", g=2, d=DH)

        TJOBS1 = [(0, 128), (256, 384), ("k0", "k1"), ("v0", "v1"), (0, 128), (256, 384), (768, 1024),
                  (1304, 1432), (1560, 1688), (1816, 1944), (2072, 2200)]
        ITEM1 = [0, 2, None, None, 4, 6, 8, 10, 12, 14, 16]
        TJOBS2 = [(0, 128), (256, 384), (512, 640), (768, 896), (1536, 1664), ("k", ),
                  (1860, 1988), (2116, 2244), (2372, 2500), (2628, 2756)]
        ITEM2 = [0, 2, 4, 6, 8, 10, 0, 2, 4, 6]

        block = ctx.enter_context(nc.Block())

        @block.sync
        def _(sp):
            def load(st, p, pieces, it=0):
                sp.wait_ge(units_split, st.freed(p, it))
                assert len(pieces) == 2
                for dst, src in pieces:
                    sp.dma_start(dst, src).then_inc(loaded[p % SLOTS], 16)

            def rows_of(w, l, r0, n, c0, m):
                return w[bass.ds(l, 1), r0:r0 + n * P, c0:c0 + m].rearrange("a (c p) m -> p (a c) m", p=P)

            def slot4(p):
                return raw[:, p % SLOTS, :].rearrange("p (c n) -> p c n", c=4)

            def slot2(p):
                return raw[:, p % SLOTS, :].rearrange("p (c n) -> p c n", c=2)

            def ffn_loads(st, l, p0, wg, up_off, wu, wd):
                def tile(t, pt, it=0):
                    for j in range(2):
                        p = pt + j
                        load(st, p, [
                            (slot4(p)[:, :, 256 * k:256 * k + 256],
                             w[bass.ds(l, 1), 512 * j:512 * j + 512, bass.ds(t * 256 + off, 256)]
                             .rearrange("a (c p) m -> p (a c) m", p=P))
                            for k, (w, off) in enumerate(((wg, 0), (wu, up_off)))], it)
                for t in range(3):
                    tile(t, p0 + 2 * t)
                with sp.Fori(0, 4) as it:
                    tile(it * 2 + 3, p0 + 6, it)
                    tile(it * 2 + 4, p0 + 8, it)
                for u in range(U_DOWN):
                    wide(st, l, p0 + U_UP + u, wd, 256 * u)

            def wide(st, l, p, w, r0):
                load(st, p, [(slot2(p)[:, c:c + 1, :], rows_of(w, l, r0 + P * c, 1, 0, DM)) for c in range(2)])

            def win_loads(st, l, p0, w, tiles):
                for n, (c0, m) in enumerate(tiles):
                    for j in range(2):
                        p = p0 + 2 * n + j
                        load(st, p, [(slot4(p)[:, 2 * h:2 * h + 2, 0:m],
                                      rows_of(w, l, 512 * j + 256 * h, 2, c0, m)) for h in range(2)])

            for i in range(2):
                sp.dma_start(x[:, i, :], I["x"][0, P * i:P * i + P, :]).then_inc(setup_loaded, 16)
            at = 0
            for name in ("norm_ffn1", "norm_mix", "norm_ffn2", "attn_norm_2", "ffn_norm_2"):
                sp.dma_start(gain_rows[at:at + L * KC, :], I[name].rearrange("l (c p) -> (l c) p", p=P))\
                    .then_inc(setup_loaded, 16)
                at += L * KC
            sp.dma_start(rot1[:, :, :], I["rot1"].rearrange("(i p) n -> p i n", p=P)).then_inc(setup_loaded, 16)
            sp.dma_start(inv_f[:, :], I["inv_freq2"].broadcast_to([P, 32])).then_inc(setup_loaded, 16)
            sp.dma_start(pos_i[:, :], I["positions_2"].rearrange("a (i p) -> p (a i)", p=P),
                         allow_slow_non_contiguous=True).then_inc(setup_loaded, 16)
            sp.dma_start(row_gain, I["norm_final"].rearrange("(a n) -> a n", a=1).broadcast_to([P, DM]))\
                .then_inc(setup_loaded, 16)

            with sp.Fori(0, L) as l:
                st = stream1(l)
                sp.wait_ge(c_evac, l * 2 + 1)
                sp.dma_start(pos_rows[0:16, :], I["pos_ck"][bass.ds(l, 1)].rearrange("a (c j) d -> (a c) (j d)", j=2))\
                    .then_inc(params1_loaded, 16)
                sp.dma_start(pos_rows[16:32, :], I["pos_cv"][bass.ds(l, 1)].rearrange("a (c j) d -> (a c) (j d)", j=2))\
                    .then_inc(params1_loaded, 16)
                for d in range(2):
                    sp.dma_start(w_k2[:, :, d, :], I["w_ck2"][bass.ds(l, 1)].rearrange("a (k p) d -> p (a k) d", p=P))\
                        .then_inc(params1_loaded, 16)
                sp.dma_start(w_v2[:, :, :], I["w_cv2"][bass.ds(l, 1)].rearrange("a (k p) d -> p (a k) d", p=P))\
                    .then_inc(params1_loaded, 16)
                ffn_loads(st, l, P1_FFN1, I["w_ffn1_gate"], 0, I["w_ffn1_up"], I["w_ffn1_down"])
                win_loads(st, l, P1_WIN, I["w_in"], WIN1)
                for u in range(4):
                    p = P1_CK + u
                    load(st, p, [(slot4(p)[:, :, 256 * k:256 * k + 256], rows_of(w, l, 512 * u, 4, 0, 256))
                                 for k, w in enumerate((I["w_ck1"], I["w_cv1"]))])
                for u in range(U_OUT):
                    wide(st, l, P1_OUT + u, I["w_out"], 256 * u)
                ffn_loads(st, l, P1_FFN2, I["w_ffn2_gate"], 0, I["w_ffn2_up"], I["w_ffn2_down"])

            with sp.Fori(0, L) as l:
                st = stream2(l)
                sp.wait_ge(c_evac, 2 * L + 1)
                sp.wait_ge(par_free, l + 1)
                at = 0
                for name, m in (("a_q_norm_2", 64), ("a_k_norm_2", 64), ("idx_k_norm_2", 64), ("b_q_norm_2", 64),
                                ("b_k_norm_2", 64), ("b_subln_2", 128), ("diff_lambda_2", 256), ("lam_init", 2)):
                    src = I[name][bass.ds(l, 1)]
                    if name == "diff_lambda_2":
                        src = src.rearrange("a b c -> a (b c)")
                    sp.dma_start(par2[:, at:at + m], src.broadcast_to([P, m])).then_inc(params2_loaded, 16)
                    at += m
                win_loads(st, l, P2_WIN, I["w_in_2"], WIN2[:2])
                sp.wait_ge(stage_T, (l * 4 + 9) * 4)
                sp.dma_start(xn[:, :, :].rearrange("p i n -> p (i n)"),
                             I["gate_bias_2"][bass.ds(l, 1)].broadcast_to([P, 2 * DM])).then_inc(bias_loaded, 16)
                win_loads(st, l, P2_WIN + 4, I["w_in_2"], WIN2[2:])
                for u in range(2):
                    wide(st, l, P2_UPA + u, I["w_up_a_2"], 256 * u)
                for u in range(2):
                    wide(st, l, P2_UPB + u, I["w_up_b_2"], 256 * u)
                for u in range(U_OUT):
                    wide(st, l, P2_OUT + u, I["w_out_2"], 256 * u)
                ffn_loads(st, l, P2_FFN, I["w_ffn_in_2"], DFF, I["w_ffn_in_2"], I["w_ffn_out_2"])

            for i in range(2):
                sp.wait_ge(x_ready, 2 * (7 + 2 * L) + i + 1)
                sp.dma_start(out[0, P * i:P * i + P, :], x[:, i, :]).then_inc(x_stored, 16)
            sp.wait_ge(x_stored, 32)

        @block.gpsimd
        def _(pool):
            def select(ap, pattern, base, fill, op):
                nc.gpsimd.drain()
                nc.gpsimd.affine_select(out=ap, in_=ap, compare_op=op, fill=fill, base=base, pattern=pattern,
                                        channel_multiplier=1)
            nc.gpsimd.memset(ident[:, :], 0.0)
            nc.gpsimd.memset(causal[:, :], 0.0)
            nc.gpsimd.memset(cmask[:, :, :], 0.0)
            nc.gpsimd.memset(cvalid[:, :, :], 1.0)
            select(ident[:, :], [[-1, P]], 0, 1.0, ALU.not_equal)
            select(causal[:, 0:P], [[-1, P]], 0, NEG, ALU.is_ge)
            select(causal[:, 2 * P:3 * P], [[-1, P]], 0, NEG, ALU.is_ge)
            select(cmask[:, :, :], [[P, 2], [-16, NCMP]], -31, NEG, ALU.is_ge)
            select(cvalid[:, :, :], [[P, 2], [-16, NCMP]], -31, 0.0, ALU.is_ge)
            nc.gpsimd.drain()
            pool.sem_inc(consts_ready, 1)

            with pool.Fori(0, L) as l:
                pool.wait_ge(proj_act, l * len(WIN1) + 2)
                pool.wait_ge(proj_dve, l * len(WIN1) + 2)
                pool.sem_inc(wait_over, 1)
                for i in range(2):
                    nc.gpsimd.tensor_copy(twice1[:, i], heads(proj1[:, i, 512:768].rearrange("p (k d) -> p k d", d=DH), 2))
                nc.gpsimd.drain()
                pool.sem_inc(twice_ready, 1)
                pool.wait_ge(tj_done, l * TJ1 + 2)
                pool.wait_ge(proj_act, l * len(WIN1) + len(WIN1))
                pool.wait_ge(proj_dve, l * len(WIN1) + len(WIN1))
                def rotate(c0, n):
                    a = proj1[:, :, c0:c0 + n * DH].rearrange("p i (h d) -> p i h d", d=DH)
                    x1, x2 = a[:, :, :, 0:8], a[:, :, :, 8:16]
                    cos, sin = heads(rot1[:, :, 0:8], n), heads(rot1[:, :, 8:16], n)
                    tmp = [row_rot[:, k, :, 0:n, :] for k in range(4)]
                    nc.gpsimd.tensor_tensor(tmp[0], x1, cos, ALU.mult)
                    nc.gpsimd.tensor_tensor(tmp[1], x2, sin, ALU.mult)
                    nc.gpsimd.tensor_tensor(tmp[2], x2, cos, ALU.mult)
                    nc.gpsimd.tensor_tensor(tmp[3], x1, sin, ALU.mult)
                    nc.gpsimd.drain()
                    nc.gpsimd.tensor_tensor(x1, tmp[0], tmp[1], ALU.subtract)
                    nc.gpsimd.tensor_tensor(x2, tmp[2], tmp[3], ALU.add)
                    nc.gpsimd.drain()
                for c0, n in ((0, 8), (768, 2), (1024, 2), (1304, 8), (1816, 8)):
                    rotate(c0, n)
                pool.sem_inc(rot_ready, 1)

        @block.scalar
        def _(act):
            def split(st, p, it=0, m=None, c=4):
                s = p % SLOTS
                act.wait_ge(loaded[s], st.loads(p, it))
                act.wait_ge(units_used, st.freed(p, it))
                src, dst = raw[:, s, :], w_hi[:, s, :]
                if m is not None:
                    src, dst = (a.rearrange("p (c n) -> p c n", c=c)[:, :, 0:m] for a in (src, dst))
                nc.scalar.activation(dst, src, ACT.Copy).then_inc(units_hi, 1)

            def norm(X):
                for i in range(2):
                    act.wait_ge(x_ready, X * 2 + (i + 1))
                    nc.scalar.activation(xn[:, i, :], x[:, i, :], ACT.Square, accum_out=ss[:, i:i + 1])
                nc.scalar.drain()
                act.sem_inc(squares, 1)

            def root(X):
                act.wait_ge(mean_sq, X + 1)
                nc.scalar.activation(rstd[:, :], ss[:, :], ACT.Sqrt).then_inc(roots, 1)

            def stage(S, gain=None):
                for b in range(4):
                    act.wait_ge(stage_T, S * 4 + (b + 1))
                    for k in range(2):
                        o = nc.scalar.activation(aT_hi[:, 2 * b + k, :], ps[:, 4 + b, SEQ * k:SEQ * k + SEQ],
                                                 ACT.Copy, scale=1.0 if gain is None else
                                                 gain_l[:, gain, 2 * b + k:2 * b + k + 1])
                    o.then_inc(stage_hi, 1)

            def ffn(st, F, p0, nxt):
                def tile(t, pt, it=0, first=False):
                    for j in range(2):
                        split(st, pt + 2 + j, it)
                    act.wait_ge(units_used, st.used(pt + 1, it))
                    b = pt // 2 - p0 // 2
                    nc.scalar.activation(sil[:, b % 2], ps[:, 2 * (b % 2):2 * (b % 2) + 2, 0:256], ACT.Silu)\
                        .then_inc(silu_done, 1)
                    if not first:
                        keep(t - 1, b + 1)

                def keep(t, b):
                    act.wait_ge(g_T, F * FT + t + 1)
                    nc.scalar.activation(gT_hi[:, bass.ds(t * 2, 2), :],
                                         ps[:, 4 + b % 2, :].rearrange("p (c n) -> p c n", c=2), ACT.Copy)\
                        .then_inc(gT_hi_done, 1)
                for t in range(3):
                    tile(t, p0 + 2 * t, first=(t == 0))
                with act.Fori(0, 4) as it:
                    tile(it * 2 + 3, p0 + 6, it)
                    tile(it * 2 + 4, p0 + 8, it)
                keep(FT - 1, FT - 1)
                for u in range(U_DOWN - 2):
                    split(st, p0 + U_UP + 2 + u)
                for args in nxt:
                    split(st, *args)

            def win(st, p0, W, tiles, nxt, gates=None):
                units = [(p0 + 2 * n + j, 0, m) for n, (_, m) in enumerate(tiles) for j in range(2)]
                for n, (c0, m) in enumerate(tiles):
                    for p, it, w in units[2 * n + 2:2 * n + 4]:
                        split(st, p, it, w)
                    if gates is None or c0 < GATES2:
                        act.wait_ge(units_used, st.used(p0 + 2 * n + 1))
                        dst, src = gates_proj(gates)[:, 0, c0:c0 + m], ps[:, 2 * (n % 2), 0:m]
                        if gates is None and n == 0:
                            dst, src = paired(dst), src.rearrange("p (g r d) -> p g r d", g=2, d=DH)
                        nc.scalar.activation(dst, src, ACT.Copy).then_inc(proj_act, 1)
                    else:
                        act.wait_ge(bias_added, gates * 4 + (n - 7 + 1))
                        nc.scalar.activation(proj2[:, :, c0:c0 + m], proj2[:, :, c0:c0 + m], ACT.Sigmoid)\
                            .then_inc(proj_act, 1)
                for args in nxt:
                    split(st, *args)

            def gates_proj(gates):
                return proj1 if gates is None else proj2

            def tj(T, k, dst):
                act.wait_ge(tj_done, T + k + 1)
                nc.scalar.activation(dst, ps[:, 4 + k % 4, 0:dst.shape[1] * SEQ]
                                     .rearrange("p (c n) -> p c n", n=SEQ), ACT.Copy).then_inc(tj_act, 1)

            def jobs(J, a, b):
                for j in range(a, b + 1):
                    if j < b:
                        act.wait_ge(scores_masked, J + j + 1)
                        if j >= a + 2:
                            act.wait_ge(probs_T, J + j - 1)
                        for i, (c, n) in enumerate(((0, P), (P, 2 * P))):
                            o = nc.scalar.activation(p_sb[:, j % 2, c:c + n], s_sb[:, j % 2, c:c + n], ACT.Exp,
                                                     bias=neg_max[:, j % 2, i:i + 1],
                                                     accum_out=sums[:, j % 4, i:i + 1])
                        nc.scalar.drain()
                        act.sem_inc(probs_ready, 1)
                    if j > a:
                        k = j - 1
                        act.wait_ge(probs_T, J + k + 1)
                        if k >= a + 2:
                            act.wait_ge(attn_done, J + k - 1)
                        nc.scalar.activation(pT_sb[:, k % 2, :], ps[:, 6 + k % 2, 0:384], ACT.Copy)\
                            .then_inc(pT_ready, 1)

            with act.Fori(0, L) as l:
                st = stream1(l)
                norm(l * 3)
                split(st, 0)
                root(l * 3)
                split(st, 1)
                stage(l * 4, 0)
                ffn(st, l * 2, P1_FFN1, [(P1_WIN, 0, 512), (P1_WIN + 1, 0, 512)])
                norm(l * 3 + 1)
                root(l * 3 + 1)
                stage(l * 4 + 1, 1)
                win(st, P1_WIN, l * 6, WIN1, [(P1_CK + k, 0, 512) for k in range(2)])
                T = l * TJ1
                tj(T, 0, tt1[:, 0:2, :])
                act.wait_ge(flat_ready, l + 1)
                for k, dst in enumerate((kflat_hi, vflat_hi)):
                    o = nc.scalar.activation(dst[:, 0:480], att[:, 992 + 480 * k:992 + 480 * k + 480], ACT.Copy)
                o.then_inc(flat_hi_done, 1)
                split(st, P1_CK + 2)
                split(st, P1_CK + 3)
                nc.scalar.drain()
                act.wait_ge(proj_dve, l * 6 + 6)
                nc.scalar.activation(gates1[:, :, :], proj1[:, :, 1280:1304], ACT.Sigmoid).then_inc(gates_done, 1)
                act.wait_ge(units_used, st.used(P1_CK + 3))
                nc.scalar.activation(h1, ps[0:30, 0:2, 0:256], ACT.Gelu_apprx_tanh).then_inc(gelu_done, 1)
                act.wait_ge(cs_shifted, l + 1)
                nc.scalar.activation(cex, csc, ACT.Exp, scale=DH ** -0.5).then_inc(c_exp, 1)
                for i in range(2):
                    act.wait_ge(c_T, l * 4 + 2 * i + 1)
                    nc.scalar.activation(pcT[0:NCMP, 0:4, :], ps[0:NCMP, 4 + 2 * i, :]
                                         .rearrange("p (h n) -> p h n", h=4), ACT.Copy).then_inc(cT_ready, 1)
                    if i == 0:
                        act.wait_ge(c_out, l * 2 + 1)
                for k in (4, 6, 8, 10):
                    tj(T, k, tt1[:, ITEM1[k]:ITEM1[k] + 2, :])
                for p in range(4):
                    split(st, P1_OUT + p)
                jobs(l * JOBS1, 0, JOBS1)
                stage(l * 4 + 2)
                norm(l * 3 + 2)
                split(st, P1_FFN2)
                root(l * 3 + 2)
                split(st, P1_FFN2 + 1)
                stage(l * 4 + 3, 2)
                ffn(st, l * 2 + 1, P1_FFN2, [])
            norm(6)
            root(6)

            for n in range(2):
                act.wait_ge(rope_arg, n + 1)
                nc.scalar.activation(cs2[:, n, :, :], att[:, 64 * n:64 * n + 64].rearrange("p (i f) -> p i f", i=2),
                                     ACT.Sin).then_inc(rope_sin, 1)

            with act.Fori(0, L) as l:
                st = stream2(l)
                norm(l * 2 + 7)
                split(st, 0)
                root(l * 2 + 7)
                split(st, 1)
                stage(l * 4 + 8, 0)
                win(st, P2_WIN, l * 11 + 12, WIN2, [(P2_UPA, ), (P2_UPA + 1, )], gates=l)
                act.wait_ge(lam_sums, l + 1)
                nc.scalar.activation(lam[:, 0:2], lam[:, 0:2], ACT.Exp).then_inc(lam_exp, 1)
                nc.scalar.drain()
                act.wait_ge(proj_dve, l * 11 + (12 + 11))
                sq = att[:, 0:2048].rearrange("p (i n) -> p i n", i=2)
                nc.scalar.activation(sq, proj2[:, :, 0:1024], ACT.Square).then_inc(head_sq, 1)
                act.wait_ge(head_sq_used, l * 2 + 1)
                nc.scalar.activation(sq, proj2[:, :, 1860:2884], ACT.Square).then_inc(head_sq, 1)
                for i in range(2):
                    nc.scalar.activation(att[:, 2048 + 64 * i:2112 + 64 * i], proj2[:, i, 1792:1856], ACT.Square,
                                         accum_out=ms[:, 64 + i:65 + i])
                nc.scalar.drain()
                act.sem_inc(head_sq, 1)
                act.wait_ge(head_ms, l + 1)
                nc.scalar.activation(ms[:, :], ms[:, :], ACT.Sqrt).then_inc(head_root, 1)
                T = l * TJ2 + TJ1 * L
                for k in (0, 2, 4):
                    tj(T, k, tt2[:, ITEM2[k]:ITEM2[k] + 2, :])
                for h in range(4):
                    act.wait_ge(idx_done, l * 4 + h + 1)
                    if h >= 2:
                        act.wait_ge(idx_used, l * 4 + h - 1)
                    nc.scalar.activation(s_sb[:, h % 2, :], ps[:, 4 + h % 2, 0:384], ACT.Relu, scale=DH ** -0.5)\
                        .then_inc(idx_relu, 1)
                for p in range(2):
                    split(st, P2_UPB + p)
                J = l * JOBS2 + JOBS1 * L
                jobs(J, 0, 8)
                for k in (6, 8):
                    tj(T, k, tt2[:, ITEM2[k]:ITEM2[k] + 2, :])
                jobs(J, 8, 16)
                act.wait_ge(yb_ms, l + 1)
                nc.scalar.activation(ms[:, 0:8], ms[:, 0:8], ACT.Sqrt).then_inc(yb_root, 1)
                stage(l * 4 + 9)
                split(st, P2_OUT)
                split(st, P2_OUT + 1)
                stage(l * 4 + 10)
                for p in range(2, 4):
                    split(st, P2_OUT + p)
                norm(l * 2 + 8)
                split(st, P2_FFN)
                root(l * 2 + 8)
                split(st, P2_FFN + 1)
                stage(l * 4 + 11, 1)
                ffn(st, l + 4, P2_FFN, [])

        @block.vector
        def _(dve):
            V = nc.vector

            def split(st, p, it=0, m=None, c=4):
                s = p % SLOTS
                dve.wait_ge(units_hi, st.index(p, it) + 1)
                a, h, o = raw[:, s, :], w_hi[:, s, :].bitcast(F32), w_lo[:, s, :]
                if m is not None:
                    a, h, o = (v.rearrange("p (c n) -> p c n", c=c)[:, :, 0:m] for v in (a, h, o))
                V.tensor_tensor(o, a, h, ALU.subtract).then_inc(units_split, 1)

            def norm(X, gain=None):
                dve.wait_ge(squares, X + 1)
                V.tensor_scalar(ss[:, :], ss[:, :], 1.0 / DM, EPS, ALU.mult, ALU.add).then_inc(mean_sq, 1)
                dve.wait_ge(roots, X + 1)
                V.reciprocal(rstd[:, :], rstd[:, :])
                V.drain()
                for i in range(2):
                    if gain is None:
                        V.tensor_scalar(xn[:, i, :], x[:, i, :], rstd[:, i:i + 1], None, ALU.mult)\
                            .then_inc(xn_ready, 1)
                    else:
                        V.scalar_tensor_tensor(x[:, i, :], x[:, i, :], rstd[:, i:i + 1], gain, ALU.mult, ALU.mult)\
                            .then_inc(x_ready, 1)

            def stage(S, gain=None):
                for b in range(4):
                    dve.wait_ge(stage_hi, S * 4 + (b + 1))
                    for k in range(2):
                        c = 2 * b + k
                        src = ps[:, 4 + b, SEQ * k:SEQ * k + SEQ]
                        hi = aT_hi[:, c, :].bitcast(F32)
                        if gain is None:
                            o = V.tensor_tensor(aT_lo[:, c, :], src, hi, ALU.subtract)
                        else:
                            o = V.scalar_tensor_tensor(aT_lo[:, c, :], src, gain_l[:, gain, c:c + 1], hi,
                                                       ALU.mult, ALU.subtract)
                    o.then_inc(stage_ready, 1)

            def residual(st, R, p_last, scale):
                for i in range(2):
                    if i == 0:
                        dve.wait_ge(down_done, R + 1)
                    else:
                        dve.wait_ge(units_used, st.used(p_last))
                    for n in range(2):
                        xs = x[:, i, 512 * n:512 * n + 512]
                        o = V.scalar_tensor_tensor(xs, ps[:, 2 * i + n, :], scale, xs, ALU.mult, ALU.add)
                    o.then_inc(x_ready, 1)

            def ffn(st, F, R, p0, nxt, scale=0.5):
                def tile(t, pt, it=0, first=False):
                    for j in range(2):
                        split(st, pt + 2 + j, it)
                    b = pt // 2 - p0 // 2
                    dve.wait_ge(silu_done, F * FT + t + 1)
                    V.tensor_tensor(gg[:, b % 2], sil[:, b % 2], ps[:, 2 * (b % 2):2 * (b % 2) + 2, 256:512],
                                    ALU.mult).then_inc(g_ready, 1)
                    if not first:
                        keep(t - 1, b + 1)

                def keep(t, b):
                    dve.wait_ge(gT_hi_done, F * FT + t + 1)
                    V.tensor_tensor(gT_lo[:, bass.ds(t * 2, 2), :],
                                    ps[:, 4 + b % 2, :].rearrange("p (c n) -> p c n", c=2),
                                    gT_hi[:, bass.ds(t * 2, 2), :].bitcast(F32), ALU.subtract).then_inc(gT_ready, 1)
                for t in range(3):
                    tile(t, p0 + 2 * t, first=(t == 0))
                with dve.Fori(0, 4) as it:
                    tile(it * 2 + 3, p0 + 6, it)
                    tile(it * 2 + 4, p0 + 8, it)
                keep(FT - 1, FT - 1)
                for u in range(U_DOWN - 2):
                    split(st, p0 + U_UP + 2 + u)
                for args in nxt:
                    split(st, *args)
                residual(st, R, p0 + U_UP + U_DOWN - 1, scale)

            def win(st, p0, W, tiles, nxt, gates=None):
                units = [(p0 + 2 * n + j, 0, m) for n, (_, m) in enumerate(tiles) for j in range(2)]
                for n, (c0, m) in enumerate(tiles):
                    for args in units[2 * n + 2:2 * n + 4]:
                        split(st, *args)
                    dve.wait_ge(units_used, st.used(p0 + 2 * n + 1))
                    if gates is None:
                        dst, src = proj1[:, 1, c0:c0 + m], ps[:, 2 * (n % 2) + 1, 0:m]
                        if n == 0:
                            dst, src = paired(dst), src.rearrange("p (g r d) -> p g r d", g=2, d=DH)
                        V.tensor_copy(dst, src).then_inc(proj_dve, 1)
                    elif c0 < GATES2:
                        V.tensor_copy(proj2[:, 1, c0:c0 + m], ps[:, 2 * (n % 2) + 1, 0:m]).then_inc(proj_dve, 1)
                    else:
                        g = n - 7
                        if g == 0:
                            dve.wait_ge(bias_loaded, (gates + 1) * 16)
                        bias = xn[:, :, :].rearrange("p i n -> p (i n)")[:, 512 * g:512 * g + 512]
                        for i in range(2):
                            o = V.tensor_tensor(proj2[:, i, c0:c0 + m], ps[:, 2 * (n % 2) + i, :], bias, ALU.add)
                        V.drain()
                        dve.sem_inc(bias_added, 1)
                        dve.sem_inc(proj_dve, 1)
                for args in nxt:
                    split(st, *args)

            def tj(T, k, dst):
                dve.wait_ge(tj_done, T + k + 1)
                V.tensor_copy(dst, ps[:, 4 + k % 4, 0:dst.shape[1] * SEQ].rearrange("p (c n) -> p c n", n=SEQ))\
                    .then_inc(tj_dve, 1)

            def jobs(J, a, b, job, mask, block2=False):
                for j in range(a, b + 2):
                    if j < b:
                        dve.wait_ge(scores_done, J + j + 1)
                        if j >= a + 2:
                            dve.wait_ge(probs_ready, J + j - 1)
                        dve.sem_inc(wait_over, 1)
                        for i, (c, n) in enumerate(((0, P), (P, 2 * P))):
                            V.tensor_tensor_reduce(out=s_sb[:, j % 2, c:c + n], in0=ps[:, 4 + j % 2, c:c + n],
                                                   in1=mask[:, c:c + n], scale=DH ** -0.5, scalar=-3.0e38,
                                                   op0=ALU.add, op1=ALU.max, accum_out=neg_max[:, j % 2, i:i + 1])
                        V.drain()
                        V.tensor_scalar(neg_max[:, j % 2, :], neg_max[:, j % 2, :], -1.0, None, ALU.mult)\
                            .then_inc(scores_masked, 1)
                    if j >= a + 2:
                        k = j - 2
                        _, _, _, _, m, o0, gate = job(k)
                        dve.wait_ge(attn_done, J + k + 1)
                        V.reciprocal(factor[:, :], sums[:, k % 4, :])
                        V.drain()
                        add = False
                        if not block2 and gate is not None:
                            V.tensor_tensor(factor[:, :], factor[:, :], gates1[:, :, gate], ALU.mult)
                            V.drain()
                            add = True
                        if block2 and gate == 1:
                            V.tensor_scalar(factor[:, :], factor[:, :], lam[:, 2:3], None, ALU.mult)
                            V.drain()
                            add = True
                        for i in range(2):
                            o = xn[:, i, o0:o0 + m]
                            src = ps[:, 2 + k % 2, P * i:P * i + m]
                            if add:
                                V.scalar_tensor_tensor(o, src, factor[:, i:i + 1], o, ALU.mult, ALU.add)
                            else:
                                V.tensor_scalar(o, src, factor[:, i:i + 1], None, ALU.mult)
                        V.drain()
                        dve.sem_inc(attn_evac, 1)

            dve.sem_inc(units_split, SLOTS)
            dve.sem_inc(par_free, 1)
            dve.sem_inc(c_evac, 1)
            dve.wait_ge(setup_loaded, 16 * 11)
            dve.wait_ge(gains_T, 1)
            V.tensor_copy(gain_cols[:, :], ps[:, 0, 0:80]).then_inc(gains_ready, 1)
            V.drain()
            dve.sem_inc(x_ready, 2)

            with dve.Fori(0, L) as l:
                st = stream1(l)
                for k in range(3):
                    V.tensor_copy(gain_l[:, k, :], gain_cols[:, bass.ds(l * KC + 16 * k, KC)])
                V.drain()
                norm(l * 3)
                split(st, 0)
                split(st, 1)
                stage(l * 4, 0)
                ffn(st, l * 2, l * 3, P1_FFN1, [(P1_WIN, 0, 512), (P1_WIN + 1, 0, 512)])
                norm(l * 3 + 1)
                stage(l * 4 + 1, 1)
                for t in (kflat_hi, kflat_lo, vflat_hi, vflat_lo):
                    V.memset(t[:, 480:578].bitcast(F32), 0.0)
                win(st, P1_WIN, l * 6, WIN1, [(P1_CK, 0, 512), (P1_CK + 1, 0, 512)])
                dve.wait_ge(pos_T, l + 1)
                V.tensor_copy(posT[:, :], ps[:, 0, 0:32])
                V.drain()
                T = l * TJ1
                tj(T, 1, tt1[:, 2:4, :])
                for k in range(2):
                    dve.wait_ge(tj_done, T + 2 + k + 1)
                    src = ps[:, 6 + k, :].rearrange("p (g t) -> p g t", g=2)
                    for g in range(2):
                        for j in range(2):
                            q = slice(DH * j, DH * j + DH)
                            for half in range(2):
                                tok = src[q, g, 16 * half:16 * half + 240].rearrange("p (n c) -> p c n", c=16)
                                tok = tok[:, j::2, :]
                                pos = posT[q, 16 * k + 8 * half:16 * k + 8 * half + 8]
                                o = V.tensor_tensor(flat[q, k, 8 * half:8 * half + 8, g, :], tok, lanes(pos, NCMP),
                                                    ALU.add)
                    o.then_inc(tj_dve, 1)
                V.drain()
                dve.sem_inc(flat_ready, 1)
                dve.wait_ge(flat_hi_done, l + 1)
                for k, (h, lo) in enumerate(((kflat_hi, kflat_lo), (vflat_hi, vflat_lo))):
                    o = V.tensor_tensor(lo[:, 0:480], att[:, 992 + 480 * k:992 + 480 * k + 480],
                                        h[:, 0:480].bitcast(F32), ALU.subtract)
                o.then_inc(flat_lo_done, 1)
                split(st, P1_CK + 2)
                split(st, P1_CK + 3)
                dve.wait_ge(h1_T, l + 1)
                V.tensor_copy(h1T[:, :, :], ps[:, 2, 0:128].rearrange("p (k n) -> p k n", k=4)[:, :, 0:30])\
                    .then_inc(h1T_ready, 1)
                dve.wait_ge(kv_c, l + 1)
                V.tensor_copy(kcT[:, :], ps[:, 3, 0:30])
                V.tensor_copy(vc[0:NCMP, :, :], ps[0:NCMP, 3, 64:192].rearrange("p (g d) -> p g d", g=2))
                V.drain()
                dve.sem_inc(kv_c_ready, 1)
                dve.wait_ge(cs_done, l + 1)
                for i in range(2):
                    for g in range(2):
                        V.tensor_tensor(csc[:, i, 4 * g:4 * g + 4],
                                        ps[:, g, 64 * i:64 * i + 64].rearrange("p (h n) -> p h n", h=4)[:, :, 0:NCMP],
                                        heads(cmask[:, i, :], 4), ALU.add)
                V.drain()
                flat_csc = att[:, 0:240].rearrange("p (h n) -> p h n", n=NCMP)
                flat_cex = att[:, 240:480].rearrange("p (h n) -> p h n", n=NCMP)
                V.tensor_reduce(cmp_max[:, :], flat_csc, AX.X, ALU.max)
                V.drain()
                V.tensor_tensor(flat_csc, flat_csc, lanes(cmp_max[:, :], NCMP), ALU.subtract).then_inc(cs_shifted, 1)
                dve.wait_ge(c_exp, l + 1)
                for i in range(2):
                    V.tensor_tensor(cex[:, i], cex[:, i], heads(cvalid[:, i, :], 8), ALU.mult)
                V.drain()
                V.tensor_reduce(cmp_max[:, :], flat_cex, AX.X, ALU.add)
                V.drain()
                V.tensor_scalar(cmp_max[:, :], cmp_max[:, :], 1.0, None, ALU.max)
                V.drain()
                V.reciprocal(cmp_max[:, :], cmp_max[:, :])
                V.drain()
                V.tensor_tensor(flat_cex, flat_cex, lanes(cmp_max[:, :], NCMP), ALU.mult).then_inc(c_probs, 1)
                dve.wait_ge(gates_done, l + 1)
                for i in range(2):
                    dve.wait_ge(c_T, l * 4 + 2 * i + 2)
                    V.tensor_copy(pcT[0:NCMP, 4:8, :], ps[0:NCMP, 5 + 2 * i, :].rearrange("p (h n) -> p h n", h=4))\
                        .then_inc(cT_ready, 1)
                    dve.wait_ge(c_out, l * 2 + i + 1)
                    V.tensor_tensor(xn[:, i, 0:512].rearrange("p (h d) -> p h d", d=DH),
                                    ps[:, 1 + i, :].rearrange("p (h d) -> p h d", d=DH),
                                    lanes(gates1[:, i, 0:24:3], DH), ALU.mult)
                    V.drain()
                    dve.sem_inc(c_evac, 1)
                for k in (5, 7, 9):
                    tj(T, k, tt1[:, ITEM1[k]:ITEM1[k] + 2, :])
                for p in range(4):
                    split(st, P1_OUT + p)
                jobs(l * JOBS1, 0, JOBS1, job1, causal)
                dve.sem_inc(xn_ready, 2)
                stage(l * 4 + 2)
                residual(st, l * 3 + 1, P1_OUT + U_OUT - 1, 1.0)
                norm(l * 3 + 2)
                split(st, P1_FFN2)
                split(st, P1_FFN2 + 1)
                stage(l * 4 + 3, 2)
                ffn(st, l * 2 + 1, l * 3 + 2, P1_FFN2, [])
            norm(6, gain=row_gain)

            C1 = 6.28125
            C2 = float(np.float32(np.round((2 * math.pi - C1) * 2.0 ** 19) / 2.0 ** 19))
            C3 = float(np.float32(2 * math.pi - C1 - C2))
            MAGIC = 12582912.0
            V.tensor_copy(pos_f[:, :], pos_i[:, :])
            V.drain()
            ang = att[:, 128:192].rearrange("p (i f) -> p i f", i=2)
            turns = att[:, 192:256]
            for i in range(2):
                V.tensor_scalar(ang[:, i, :], inv_f[:, :], pos_f[:, i:i + 1], None, ALU.mult)
            V.drain()
            for n, (turn, shift) in enumerate(((0.25, math.pi / 2), (0.0, 0.0))):
                r = att[:, 64 * n:64 * n + 64]
                V.tensor_scalar(turns, att[:, 128:192], 1.0 / (2 * math.pi), turn, ALU.mult, ALU.add)
                V.drain()
                V.tensor_scalar(turns, turns, MAGIC, None, ALU.add)
                V.drain()
                V.tensor_scalar(turns, turns, MAGIC, None, ALU.subtract)
                V.drain()
                V.scalar_tensor_tensor(r, turns, -C1, att[:, 128:192], ALU.mult, ALU.add)
                V.drain()
                V.scalar_tensor_tensor(r, turns, -C2, r, ALU.mult, ALU.add)
                V.drain()
                V.scalar_tensor_tensor(r, turns, -C3, r, ALU.mult, ALU.add)
                V.drain()
                V.tensor_scalar(r, r, shift, 3.1415925, ALU.add, ALU.min)
                V.drain()
                V.tensor_scalar(r, r, -3.1415925, None, ALU.max).then_inc(rope_arg, 1)
            dve.wait_ge(rope_sin, 2)

            with dve.Fori(0, L) as l:
                st = stream2(l)
                for k in range(2):
                    V.tensor_copy(gain_l[:, k, :], gain_cols[:, bass.ds(l * KC + 48 + 16 * k, KC)])
                V.drain()
                norm(l * 2 + 7)
                split(st, 0)
                split(st, 1)
                stage(l * 4 + 8, 0)
                dve.wait_ge(params2_loaded, (l + 1) * 128)
                for n in range(5):
                    g = par2[:, 64 * n:64 * n + 64]
                    for k, (trig, half) in enumerate(((0, 0), (1, 1), (0, 1), (1, 0))):
                        V.tensor_tensor(rg[:, n, k], cs2[:, trig],
                                        heads(g[:, 32 * half:32 * half + 32], 2), ALU.mult)
                dl = par2[:, 448:704].rearrange("p (a b d) -> p a b d", a=2, b=2)
                V.tensor_tensor(score[:, 0:128].rearrange("p (a d) -> p a d", a=2), dl[:, :, 0, :], dl[:, :, 1, :],
                                ALU.mult)
                V.drain()
                V.tensor_reduce(lam[:, 0:2], score[:, 0:128].rearrange("p (a d) -> p a d", a=2), AX.X, ALU.add)\
                    .then_inc(lam_sums, 1)
                V.tensor_scalar(par2[:, 320:448], par2[:, 320:448], par2[:, 705:706], None, ALU.mult)
                win(st, P2_WIN, l * 11 + 12, WIN2, [(P2_UPA, ), (P2_UPA + 1, )], gates=l)
                dve.wait_ge(lam_exp, l + 1)
                V.tensor_tensor(lam[:, 2:3], lam[:, 1:2], lam[:, 0:1], ALU.subtract)
                V.drain()
                V.tensor_tensor(lam[:, 2:3], lam[:, 2:3], par2[:, 704:705], ALU.subtract)
                for n in range(2):
                    dve.wait_ge(head_sq, l * 3 + n + 1)
                    V.tensor_reduce(ms[:, 32 * n:32 * n + 32], att[:, 0:2048].rearrange("p (h d) -> p h d", d=DH),
                                    AX.X, ALU.add).then_inc(head_sq_used, 1)
                V.drain()
                dve.wait_ge(head_sq, l * 3 + 3)
                V.tensor_scalar(ms[:, :], ms[:, :], 1.0 / DH, EPS, ALU.mult, ALU.add).then_inc(head_ms, 1)
                dve.wait_ge(head_root, l + 1)
                V.reciprocal(ms[:, :], ms[:, :])
                V.tensor_scalar(iw[:, :, :], proj2[:, :, 1856:1860], 0.5, None, ALU.mult)
                V.drain()

                def rotate(c0, n, tabs, scale):
                    a = proj2[:, :, c0:c0 + n * DH].rearrange("p i (h d) -> p i h d", d=DH)
                    x1, x2 = a[:, :, :, 0:32], a[:, :, :, 32:64]
                    tmp = [att[:, 512 * k:512 * k + 64 * n].rearrange("p (i h d) -> p i h d", i=2, d=32)
                           for k in range(4)]
                    for k, v in enumerate((x1, x2, x2, x1)):
                        V.tensor_tensor(tmp[k], v, heads(tabs[k], n), ALU.mult)
                    V.drain()
                    V.tensor_tensor(x1, tmp[0], tmp[1], ALU.subtract)
                    V.tensor_tensor(x2, tmp[2], tmp[3], ALU.add)
                    V.drain()
                    if scale is not None:
                        for i in range(2):
                            V.tensor_tensor(a[:, i], a[:, i], lanes(scale[:, i, :], DH), ALU.mult)
                    V.drain()
                msA = ms[:, 0:32].rearrange("p (i h) -> p i h", i=2)
                msB = ms[:, 32:64].rearrange("p (i h) -> p i h", i=2)
                msI = ms[:, 64:66].rearrange("p (i h) -> p i h", i=2)
                rotate(0, 8, [rg[:, 0, k] for k in range(4)], msA[:, :, 0:8])
                rotate(512, 8, [rg[:, 1, k] for k in range(4)], msA[:, :, 8:16])
                rotate(1536, 4, [cs2[:, 0], cs2[:, 1], cs2[:, 0], cs2[:, 1]], None)
                rotate(1792, 1, [rg[:, 2, k] for k in range(4)], msI)
                V.tensor_copy(twice2, heads(proj2[:, :, 1792:1856], 2))
                V.drain()
                dve.sem_inc(rot_ready, 1)
                rotate(1860, 8, [rg[:, 3, k] for k in range(4)], msB[:, :, 0:8])
                rotate(2372, 8, [rg[:, 4, k] for k in range(4)], msB[:, :, 8:16])
                T = l * TJ2 + TJ1 * L
                tj(T, 1, tt2[:, 2:4, :])
                tj(T, 3, tt2[:, 6:8, :])
                tj(T, 5, tt2[:, 10:11, :])
                for h in range(4):
                    dve.wait_ge(idx_relu, l * 4 + h + 1)
                    for i, (c, n) in enumerate(((0, P), (P, 2 * P))):
                        V.scalar_tensor_tensor(score[:, c:c + n], s_sb[:, h % 2, c:c + n], iw[:, i, h:h + 1],
                                               (causal if h == 0 else score)[:, c:c + n], ALU.mult, ALU.add)
                    V.drain()
                    dve.sem_inc(idx_used, 1)
                for _ in range(8):
                    for i, (c, n) in enumerate(((0, P), (P, 2 * P))):
                        V.max(m8[:, i, :], score[:, c:c + n])
                    V.drain()
                    for i, (c, n) in enumerate(((0, P), (P, 2 * P))):
                        V.match_replace(score[:, c:c + n], m8[:, i, :], score[:, c:c + n], TAKEN)
                    V.drain()
                V.tensor_scalar(score[:, :], score[:, :], TAKEN, NEG, ALU.not_equal, ALU.mult)
                V.drain()
                V.tensor_tensor(score[:, :], score[:, :], causal[:, :], ALU.add)
                V.drain()
                for p in range(2):
                    split(st, P2_UPB + p)
                J = l * JOBS2 + JOBS1 * L
                jobs(J, 0, 8, job2, score, True)
                for k in (7, 9):
                    tj(T, k, tt2[:, ITEM2[k]:ITEM2[k] + 2, :])
                jobs(J, 8, 16, job2, causal, True)
                yb = xn[:, :, 512:1024].rearrange("p i (h d) -> p i h d", d=P)
                sq = att[:, 0:1024].rearrange("p (i h d) -> p i h d", i=2, d=P)
                for i in range(2):
                    V.tensor_tensor(sq[:, i], yb[:, i], yb[:, i], ALU.mult)
                V.drain()
                V.tensor_reduce(ms[:, 0:8], att[:, 0:1024].rearrange("p (h d) -> p h d", d=P), AX.X, ALU.add)
                V.drain()
                V.tensor_scalar(ms[:, 0:8], ms[:, 0:8], 1.0 / P, EPS, ALU.mult, ALU.add).then_inc(yb_ms, 1)
                dve.wait_ge(yb_root, l + 1)
                V.reciprocal(ms[:, 0:8], ms[:, 0:8])
                V.drain()
                for i in range(2):
                    V.tensor_tensor(yb[:, i], yb[:, i], lanes(ms[:, 4 * i:4 * i + 4], P), ALU.mult)
                V.drain()
                for i in range(2):
                    V.tensor_tensor(yb[:, i], yb[:, i], heads(par2[:, 320:448], 4), ALU.mult)\
                        .then_inc(xn_ready, 1)
                V.drain()
                dve.sem_inc(par_free, 1)
                stage(l * 4 + 9)
                split(st, P2_OUT)
                split(st, P2_OUT + 1)
                dve.wait_ge(units_used, st.used(P2_UPA + 1))
                for i in range(2):
                    V.tensor_tensor(xn[:, i, :].rearrange("p (n c) -> p n c", n=2), ps[:, 2 * i:2 * i + 2, :],
                                    proj2[:, i, GATES2:GATES2 + DM].rearrange("p (n c) -> p n c", n=2), ALU.mult)
                dve.wait_ge(units_used, st.used(P2_UPB + 1))
                for i in range(2):
                    gb = proj2[:, i, GATES2 + DM:GATES2 + 2 * DM]
                    V.tensor_tensor(gb.rearrange("p (n c) -> p n c", n=2), ps[:, 4 + 2 * i:6 + 2 * i, :],
                                    gb.rearrange("p (n c) -> p n c", n=2), ALU.mult)
                V.drain()
                for i in range(2):
                    gb = proj2[:, i, GATES2 + DM:GATES2 + 2 * DM]
                    V.tensor_tensor(xn[:, i, :], xn[:, i, :], gb, ALU.add).then_inc(xn_ready, 1)
                stage(l * 4 + 10)
                for p in range(2, 4):
                    split(st, P2_OUT + p)
                residual(st, l * 2 + 6, P2_OUT + U_OUT - 1, 1.0)
                norm(l * 2 + 8)
                split(st, P2_FFN)
                split(st, P2_FFN + 1)
                stage(l * 4 + 11, 1)
                ffn(st, l + 4, l * 2 + 7, P2_FFN, [], scale=1.0)

        @block.tensor
        def _(pe):
            M = nc.tensor.matmul

            def three(o, ah, al, wh, wl, start, stop):
                M(o, ah, wh, start=start, stop=False)
                M(o, ah, wl, start=False, stop=False)
                return M(o, al, wh, start=False, stop=stop)

            def split_ready(st, p, it=0):
                pe.wait_ge(units_split, st.index(p, it) + (1 + SLOTS))

            def stage(S):
                pe.wait_ge(xn_ready, S * 2 + 2)
                for b in range(4):
                    for k in range(2):
                        for i in range(2):
                            c = 2 * b + k
                            o = nc.tensor.transpose(ps[:, 4 + b, SEQ * k + P * i:SEQ * k + P * i + P],
                                                    xn[:, i, P * c:P * c + P], ident[:, :])
                    o.then_inc(stage_T, 1)

            def full_k(st, S, pt, it, bank, m):
                for j in range(2):
                    p = pt + j
                    split_ready(st, p, it)
                    if S is not None:
                        pe.wait_ge(stage_ready, S * 4 + 2 * j + 2)
                    for i in range(2):
                        for c in range(4):
                            k = 4 * j + c
                            o = three(ps[:, bank + i, 0:m], aT_hi[:, k, P * i:P * i + P], aT_lo[:, k, P * i:P * i + P],
                                      w_hi[:, p % SLOTS, 512 * c:512 * c + m], w_lo[:, p % SLOTS, 512 * c:512 * c + m],
                                      k == 0, k == KC - 1)
                    if j == 0:
                        o.then_inc(units_used, 1)
                return o

            def wide(st, p, u, last, src_hi, src_lo, k0, bank=0, done=None):
                split_ready(st, p)
                for i in range(2):
                    for n in range(2):
                        for c in range(2):
                            k = k0 + c
                            w = 1024 * c + 512 * n
                            o = three(ps[:, bank + 2 * i + n, :], src_hi[:, k, P * i:P * i + P],
                                      src_lo[:, k, P * i:P * i + P], w_hi[:, p % SLOTS, w:w + 512],
                                      w_lo[:, p % SLOTS, w:w + 512], u == 0 and c == 0, last and c == 1)
                    if last and done is not None and i == 0:
                        o.then_inc(done, 1)
                return o

            def ffn(st, F, S, p0):
                def tile(t, pt, it=0, stat=None):
                    b = pt // 2 - p0 // 2
                    if stat is None or stat >= 2:
                        pe.wait_ge(g_ready, F * FT + t - 1)
                    o = full_k(st, S if stat == 0 else None, pt, it, 2 * (b % 2), 512)
                    o.then_inc(units_used, 1)

                def turn(t, b, stat=None):
                    pe.wait_ge(g_ready, F * FT + t + 1)
                    if stat is None or stat >= 2:
                        pe.wait_ge(gT_ready, F * FT + t - 1)
                    for c in range(2):
                        for i in range(2):
                            o = nc.tensor.transpose(ps[:, 4 + b % 2, SEQ * c + P * i:SEQ * c + P * i + P],
                                                    gg[:, b % 2, i, P * c:P * c + P], ident[:, :])
                    o.then_inc(g_T, 1)

                def both(t, pt, it=0, stat=None):
                    tile(t, pt, it, stat)
                    b = pt // 2 - p0 // 2
                    if stat is None or stat >= 1:
                        turn(t - 1, b + 1, None if stat is None else stat - 1)
                for t in range(3):
                    both(t, p0 + 2 * t, 0, t)
                with pe.Fori(0, 4) as it:
                    both(it * 2 + 3, p0 + 6, it)
                    both(it * 2 + 4, p0 + 8, it)
                turn(FT - 1, FT - 1)
                for u in range(U_DOWN):
                    pe.wait_ge(gT_ready, F * FT + u + 1)
                    o = wide(st, p0 + U_UP + u, u, u == U_DOWN - 1, gT_hi, gT_lo, 2 * u, done=down_done)
                    o.then_inc(units_used, 1)

            def out_proj(st, S, p0):
                for u in range(U_OUT):
                    if u % 2 == 0:
                        pe.wait_ge(stage_ready, S * 4 + u + 2)
                    o = wide(st, p0 + u, u, u == U_OUT - 1, aT_hi, aT_lo, 2 * u, done=down_done)
                    o.then_inc(units_used, 1)

            def win(st, S, p0, W, tiles):
                for n, (c0, m) in enumerate(tiles):
                    if n >= 2:
                        pe.wait_ge(proj_act, W + n - 1)
                        pe.wait_ge(proj_dve, W + n - 1)
                    o = full_k(st, S if n == 0 else None, p0 + 2 * n, 0, 2 * (n % 2), m)
                    o.then_inc(units_used, 1)

            def tjobs(T, ks, jobs, src, kfree):
                for k in ks:
                    kfree(k)
                    for e, c0 in enumerate(jobs[k]):
                        for i in range(2):
                            if c0 == "k":
                                block_in = twice2[:, i].rearrange("p e d -> p (e d)")
                            elif isinstance(c0, str):
                                block_in = twice1[:, i, 2 * (k - 2) + e].rearrange("p e d -> p (e d)")
                            else:
                                block_in = src[:, i, c0:c0 + P]
                            o = nc.tensor.transpose(ps[:, 4 + k % 4, SEQ * e + P * i:SEQ * e + P * i + P],
                                                    block_in, ident[:, :])
                    o.then_inc(tj_done, 1)

            def scores(qT, kT, q0, bank):
                q = slice(q0, q0 + DH)
                M(ps[:, bank, 0:P], qT[q, 0:P], kT[q, 0:P], start=True, stop=True)
                return M(ps[:, bank, P:3 * P], qT[q, P:2 * P], kT[q, :], start=True, stop=True)

            def jobs(J, a, b, job, items, src):
                for j in range(a, b + 2):
                    if j < b:
                        q0, qi, ki, v0, m, o0, _ = job(j)
                        if j >= a + 2:
                            pe.wait_ge(scores_masked, J + j - 1)
                        scores(items[:, qi, :], items[:, ki, :], q0, 4 + j % 2).then_inc(scores_done, 1)
                    if a <= j - 1 < b:
                        k = j - 1
                        pe.wait_ge(probs_ready, J + k + 1)
                        if k >= a + 2:
                            pe.wait_ge(pT_ready, J + k - 1)
                        for s in range(3):
                            o = nc.tensor.transpose(ps[:, 6 + k % 2, P * s:P * s + P], p_sb[:, k % 2, P * s:P * s + P],
                                                    ident[:, :])
                        o.then_inc(probs_T, 1)
                    if j >= a + 2:
                        k = j - 2
                        _, _, _, v0, m, _, _ = job(k)
                        pe.wait_ge(pT_ready, J + k + 1)
                        if k >= a + 2:
                            pe.wait_ge(attn_evac, J + k - 1)
                        M(ps[:, 2 + k % 2, 0:m], pT_sb[:, k % 2, 0:P], src[:, 0, v0:v0 + m], start=True, stop=True)
                        M(ps[:, 2 + k % 2, P:P + m], pT_sb[:, k % 2, P:2 * P], src[:, 0, v0:v0 + m],
                          start=True, stop=False)
                        M(ps[:, 2 + k % 2, P:P + m], pT_sb[:, k % 2, 2 * P:3 * P], src[:, 1, v0:v0 + m],
                          start=False, stop=True).then_inc(attn_done, 1)

            pe.sem_inc(units_used, SLOTS)
            pe.wait_ge(consts_ready, 1)
            pe.wait_ge(setup_loaded, 16 * 11)
            nc.tensor.transpose(ps[:, 0, 0:80], gain_rows[:, :], ident[0:80, 0:80]).then_inc(gains_T, 1)

            with pe.Fori(0, L) as l:
                st = stream1(l)
                stage(l * 4)
                ffn(st, l * 2, l * 4, P1_FFN1)
                stage(l * 4 + 1)
                win(st, l * 4 + 1, P1_WIN, l * 6, WIN1)
                pe.wait_ge(proj_act, l * 6 + 6)
                pe.wait_ge(proj_dve, l * 6 + 6)
                pe.wait_ge(params1_loaded, (l + 1) * 80)
                pe.sem_inc(wait_over, 1)
                nc.tensor.transpose(ps[:, 0, 0:32], pos_rows[:, :], ident[0:32, 0:32]).then_inc(pos_T, 1)
                pe.wait_ge(twice_ready, l + 1)
                T = l * TJ1
                tjobs(T, range(4), TJOBS1, proj1, lambda k: None)
                pe.wait_ge(flat_lo_done, l + 1)
                for u in range(4):
                    p = P1_CK + u
                    split_ready(st, p)
                    for c in range(4):
                        k = 4 * u + c
                        for n, (h, lo) in enumerate(((kflat_hi, kflat_lo), (vflat_hi, vflat_lo))):
                            w = 512 * c + 256 * n
                            o = three(ps[:, n, 0:256], h[:, 30 * k:30 * k + P], lo[:, 30 * k:30 * k + P],
                                      w_hi[:, p % SLOTS, w:w + 256], w_lo[:, p % SLOTS, w:w + 256],
                                      k == 0, k == 15)
                    o.then_inc(units_used, 1)
                pe.wait_ge(gelu_done, l + 1)
                pe.sem_inc(wait_over, 1)
                for n in range(2):
                    for k in range(2):
                        o = nc.tensor.transpose(ps[:, 2, 32 * (2 * n + k):32 * (2 * n + k) + 30],
                                                h1[:, n, P * k:P * k + P], ident[0:30, 0:30])
                o.then_inc(h1_T, 1)
                pe.wait_ge(h1T_ready, l + 1)
                for k in range(2):
                    M(ps[:, 3, 0:30], w_k2[:, k, :, :].rearrange("p a d -> p (a d)"), h1T[:, k, :],
                      start=k == 0, stop=k == 1)
                for g in range(2):
                    for k in range(2):
                        o = M(ps[0:NCMP, 3, 64 + DH * g:64 + DH * g + DH], h1T[:, 2 + k, NCMP * g:NCMP * g + NCMP],
                              w_v2[:, k, :], start=k == 0, stop=k == 1)
                o.then_inc(kv_c, 1)
                pe.wait_ge(kv_c_ready, l + 1)
                pe.wait_ge(tj_act, l * 5 + 1)
                for i in range(2):
                    for h in range(8):
                        g = h // 4
                        q = slice(DH * g, DH * g + DH)
                        at = 64 * i + 16 * (h % 4)
                        o = M(ps[:, g, at:at + NCMP], tt1[q, h % 4, P * i:P * i + P],
                              kcT[q, NCMP * g:NCMP * g + NCMP], start=True, stop=True)
                o.then_inc(cs_done, 1)
                pe.wait_ge(c_probs, l + 1)
                for i in range(2):
                    for half in range(2):
                        for h in range(4):
                            o = nc.tensor.transpose(ps[0:NCMP, 4 + 2 * i + half, P * h:P * h + P],
                                                    cex[:, i, 4 * half + h, :], ident[:, :])
                        o.then_inc(c_T, 1)
                for i in range(2):
                    pe.wait_ge(cT_ready, l * 4 + 2 * i + 2)
                    for h in range(8):
                        o = M(ps[:, 1 + i, DH * h:DH * h + DH], pcT[0:NCMP, h, :], vc[0:NCMP, h // 4, :],
                              start=True, stop=True)
                    o.then_inc(c_out, 1)
                pe.wait_ge(rot_ready, l + 1)

                def free1(k):
                    if k >= 8:
                        if k % 2 == 0:
                            pe.wait_ge(tj_act, l * 5 + (k - 4) // 2)
                        else:
                            pe.wait_ge(tj_dve, l * 6 + (3 + (k - 7) // 2))
                tjobs(T, range(4, 11), TJOBS1, proj1, free1)
                pe.wait_ge(tj_act, l * 5 + 5)
                pe.wait_ge(tj_dve, l * 6 + 6)
                jobs(l * JOBS1, 0, JOBS1, job1, tt1, proj1)
                stage(l * 4 + 2)
                out_proj(st, l * 4 + 2, P1_OUT)
                stage(l * 4 + 3)
                ffn(st, l * 2 + 1, l * 4 + 3, P1_FFN2)

            with pe.Fori(0, L) as l:
                st = stream2(l)
                stage(l * 4 + 8)
                win(st, l * 4 + 8, P2_WIN, l * 11 + 12, WIN2)
                T = l * TJ2 + TJ1 * L
                pe.wait_ge(rot_ready, l + L + 1)

                def free2(k):
                    if k == 4:
                        pe.wait_ge(tj_act, l * 5 + 11)
                    if k == 5:
                        pe.wait_ge(tj_dve, l * 5 + 13)
                tjobs(T, range(6), TJOBS2, proj2, free2)
                pe.wait_ge(tj_act, l * 5 + 13)
                pe.wait_ge(tj_dve, l * 5 + 15)
                for h in range(4):
                    if h >= 2:
                        pe.wait_ge(idx_relu, l * 4 + h - 1)
                    scores(tt2[:, 8 + h // 2, :], tt2[:, 10, :], DH * (h % 2), 4 + h % 2).then_inc(idx_done, 1)
                pe.wait_ge(idx_relu, l * 4 + 4)
                J = l * JOBS2 + JOBS1 * L
                jobs(J, 0, 8, job2, tt2, proj2)
                tjobs(T, range(6, 10), TJOBS2, proj2, lambda k: None)
                pe.wait_ge(tj_act, l * 5 + 15)
                pe.wait_ge(tj_dve, l * 5 + 17)
                jobs(J, 8, 16, job2, tt2, proj2)
                stage(l * 4 + 9)
                pe.wait_ge(stage_ready, (l * 4 + 9) * 4 + 4)
                for u in range(2):
                    wide(st, P2_UPA + u, u, u == 1, aT_hi, aT_lo, 2 * u).then_inc(units_used, 1)
                for u in range(2):
                    wide(st, P2_UPB + u, u, u == 1, aT_hi, aT_lo, 4 + 2 * u, bank=4).then_inc(units_used, 1)
                stage(l * 4 + 10)
                out_proj(st, l * 4 + 10, P2_OUT)
                stage(l * 4 + 11)
                ffn(st, l + 4, l * 4 + 11, P2_FFN)


_INS = ["x", "norm_ffn1", "w_ffn1_gate", "w_ffn1_up", "w_ffn1_down", "norm_mix", "w_in", "pos_ck", "w_ck1", "w_ck2",
        "pos_cv", "w_cv1", "w_cv2", "w_out", "norm_ffn2", "w_ffn2_gate", "w_ffn2_up", "w_ffn2_down", "norm_final",
        "positions_2", "attn_norm_2", "w_in_2", "gate_bias_2", "a_q_norm_2", "a_k_norm_2", "idx_k_norm_2",
        "b_q_norm_2", "b_k_norm_2", "diff_lambda_2", "b_subln_2", "w_up_a_2", "w_up_b_2", "w_out_2", "ffn_norm_2",
        "w_ffn_in_2", "w_ffn_out_2"]


def shape_constants():
    f = np.float32
    inv1 = np.power(f(500000.0), -(np.arange(0, 16, 2, dtype=f) / f(16))).astype(f)
    ang = np.arange(SEQ, dtype=f)[:, None] * inv1[None, :]
    inv2 = (f(1.0) / np.power(f(10000.0), np.arange(0, DH, 2, dtype=f) / f(DH))).astype(f)
    init = [0.8 - 0.6 * math.exp(-0.3 * l) for l in range(DEPTH)]
    return {"rot1": np.concatenate([np.cos(ang), np.sin(ang)], axis=1).astype(f),
            "inv_freq2": inv2[None, :],
            "lam_init": np.array([[v, 1.0 - v] for v in init], dtype=f)}


def kernel(**inputs):
    import concourse.bacc as _bacc
    from concourse.bass_utils import run_bass_kernel_spmd as _run

    nc = _bacc.Bacc("TRN2", target_bir_lowering=False, num_devices=1)
    arrays, aps = {}, {}
    given = {name: np.ascontiguousarray(inputs[name]) for name in _INS}
    given.update(shape_constants())
    for name, a in given.items():
        arrays[f"in_{name}"] = a
        aps[name] = nc.dram_tensor(f"in_{name}", a.shape, mybir.dt.from_np(a.dtype), kind="ExternalInput").ap()
    out = nc.dram_tensor("out_x", (1, SEQ, DM), F32, kind="ExternalOutput").ap()
    build(nc, aps, out)
    return _run(nc, [arrays], core_ids=[0]).results[0]["out_x"]
```

```python
import math
from contextlib import ExitStack

import concourse.bass as bass
from concourse import mybir
import numpy as np

ALU = mybir.AluOpType
ACT = mybir.ActivationFunctionType
AX = mybir.AxisListType
F32 = mybir.dt.float32
F32R = mybir.dt.float32r
I32 = mybir.dt.int32

P = 128
SEQ = 256
TT_ = SEQ // P
DM = 1024
KC = DM // P
DFF = 2816
FT = DFF // 256
DH = 64
DEPTH = 2
EPS = 1e-6
NEG = -1e30
TAKEN = -3e38
NCMP = (SEQ - 32) // 16 + 1
SLOTS = 4
UNIT = 2048

WIN1 = [(0, 512), (512, 512), (1024, 280), (1304, 512), (1816, 512), (2328, 512)]
WIN2 = [(0, 512), (512, 512), (1536, 324), (1860, 512), (2372, 512), (2884, 512), (1024, 512)] + \
       [(3396 + 512 * g, 512) for g in range(4)]
IN1 = 2840
IN2 = 5444
GATES2 = 3396

U_UP, U_DOWN, U_OUT = 2 * FT, FT, 4
P1_FFN1 = 0
P1_WIN = P1_FFN1 + U_UP + U_DOWN
P1_CK = P1_WIN + 2 * len(WIN1)
P1_OUT = P1_CK + 4
P1_FFN2 = P1_OUT + U_OUT
U1 = P1_FFN2 + U_UP + U_DOWN
P2_WIN = 0
P2_UPA = P2_WIN + 2 * len(WIN2)
P2_UPB = P2_UPA + 2
P2_OUT = P2_UPB + 2
P2_FFN = P2_OUT + U_OUT
U2 = P2_FFN + U_UP + U_DOWN

JOBS1, JOBS2 = 24, 16
TJ1, TJ2 = 11, 10
JOBS2_FROM = 13
STEPS2 = (2, 2, 2, 2, 2, 2, 3, 3, 2)
STEP_AT = {2: (3, 7), 3: (2, 5, 7)}


def slot_units(u, s):
    return (u - s + SLOTS - 1) // SLOTS


def since_slot(p, before):
    if p >= SLOTS:
        return SLOTS
    return min(min(p + u - q for q in range(u) if q % SLOTS == p % SLOTS) for u in before)


class Stream:

    def __init__(self, l, units, base_units, base_slots, before):
        self.l, self.units, self.base, self.base_slots, self.before = l, units, base_units, base_slots, before

    def index(self, p, it=0):
        return self.l * self.units + it * SLOTS + (self.base + p)

    def loads(self, p, it=0):
        s = p % SLOTS
        return (self.l * slot_units(self.units, s) + it + (self.base_slots[s] + p // SLOTS + 1)) * 32

    def used(self, p, it=0):
        return self.index(p, it) + 1 + SLOTS

    def freed(self, p, it=0):
        return self.index(p, it) + 1 + SLOTS - since_slot(p, self.before)


def stream1(l):
    return Stream(l, U1, 0, [0] * SLOTS, (U1,))


def stream2(l):
    return Stream(l, U2, DEPTH * U1, [DEPTH * slot_units(U1, s) for s in range(SLOTS)], (U1, U2))


def build(nc, I, out):
    L = DEPTH
    with ExitStack() as ctx:
        def sb(name, shape, dt=F32):
            return ctx.enter_context(nc.sbuf_tensor(name, shape, dt))

        def sem(name):
            return ctx.enter_context(nc.semaphore(name))

        raw = sb("raw", [P, SLOTS, UNIT])
        w_hi = sb("w_hi", [P, SLOTS, UNIT], F32R)
        w_lo = sb("w_lo", [P, SLOTS, UNIT], F32R)
        x = sb("x", [P, 2, DM])
        xn = sb("xn", [P, 2, DM])
        aT_hi = sb("aT_hi", [P, KC, SEQ], F32R)
        aT_lo = sb("aT_lo", [P, KC, SEQ], F32R)
        att = sb("att", [P, 2304])
        ident = sb("ident", [P, P])
        causal = sb("causal", [P, 384])
        cmask = sb("cmask", [P, 2, NCMP])
        cvalid = sb("cvalid", [P, 2, NCMP])
        gain_rows = sb("gain_rows", [80, P])
        gain_cols = sb("gain_cols", [P, 80])
        gain_l = sb("gain_l", [P, 3, KC])
        ss = sb("ss", [P, 2])
        rstd = sb("rstd", [P, 2])
        rot1 = sb("rot1", [P, 2, 16])
        neg_max = sb("neg_max", [P, 4, 2])
        sums = sb("sums", [P, 4, 2])
        with ExitStack() as r:
            row_rot = r.enter_context(nc.sbuf_tensor("row_rot", [P, 4, 2, 8, 8], F32))
        with ExitStack() as r:
            score = r.enter_context(nc.sbuf_tensor("score", [P, 384], F32))
        rot_end = sb("rot_end", [P, 512])
        factor = sb("factor", [P, 4, 2])
        with ExitStack() as r:
            gT_hi = r.enter_context(nc.sbuf_tensor("gT_hi", [P, 2 * FT, SEQ], F32R))
            gT_lo = r.enter_context(nc.sbuf_tensor("gT_lo", [P, 2 * FT, SEQ], F32R))
        with ExitStack() as r:
            def rb(name, shape, dt=F32):
                return r.enter_context(nc.sbuf_tensor(name, shape, dt))
            proj1 = rb("proj1", [P, 2, IN1])
            tt1 = rb("tt1", [P, 18, SEQ])
            kflat_hi = rb("kflat_hi", [P, 16 * 30 + 98], F32R)
            kflat_lo = rb("kflat_lo", [P, 16 * 30 + 98], F32R)
            vflat_hi = rb("vflat_hi", [P, 16 * 30 + 98], F32R)
            vflat_lo = rb("vflat_lo", [P, 16 * 30 + 98], F32R)
            pcT = rb("pcT", [16, 8, P])
        with ExitStack() as r:
            proj2 = rb("proj2", [P, 2, IN2])
            tt2 = rb("tt2", [P, 11, SEQ])
        region_end = sb("region_end", [P, 13800])
        with ExitStack() as r:
            pos_rows = r.enter_context(nc.sbuf_tensor("pos_rows", [32, P], F32))
            posT = r.enter_context(nc.sbuf_tensor("posT", [P, 32], F32))
            w_k2 = r.enter_context(nc.sbuf_tensor("w_k2", [P, 2, 2, DH], F32))
            w_v2 = r.enter_context(nc.sbuf_tensor("w_v2", [P, 2, DH], F32))
            h1T = r.enter_context(nc.sbuf_tensor("h1T", [P, 4, 30], F32))
        with ExitStack() as r:
            par2 = r.enter_context(nc.sbuf_tensor("par2", [P, 706], F32))
        par_end = sb("par_end", [P, 720])
        kcT = sb("kcT", [P, 30])
        vc = sb("vc", [16, 2, DH])
        gates1 = sb("gates1", [P, 2, 24])
        cmp_max = sb("cmp_max", [P, 16])
        pos_i = sb("pos_i", [P, 2], I32)
        pos_f = sb("pos_f", [P, 2])
        inv_f = sb("inv_f", [P, 32])
        cs2 = sb("cs2", [P, 2, 2, 32])
        rg = sb("rg", [P, 5, 4, 2, 32])
        row_gain = rg[:, :, :, :, :].rearrange("p a b c d -> p (a b c d)")[:, 0:DM]
        ms = sb("ms", [P, 66])
        lam = sb("lam", [P, 3])
        iw = sb("iw", [P, 2, 4])
        m8 = sb("m8", [P, 2, 8])

        twice1 = tt1[:, 10:14, :].rearrange("p a n -> p (a n)").rearrange("p (i k e d) -> p i k e d", i=2, k=4, e=2)
        twice2 = att[:, 2048:2304].rearrange("p (i e d) -> p i e d", i=2, e=2)
        sil = att[:, 0:1024].rearrange("p (b i n) -> p b i n", b=2, i=2)
        gg = att[:, 1024:2048].rearrange("p (b i n) -> p b i n", b=2, i=2)
        p_sb = att[:, 0:1536].rearrange("p (b n) -> p b n", b=4)
        pT_sb = att[:, 1536:2304].rearrange("p (b n) -> p b n", b=2)
        flat = att[:, 992:992 + 960].rearrange("p (k c g n) -> p k c g n", k=2, c=16, g=2)

        ps = ctx.enter_context(nc.psum_tensor("ps", [P, 8, 512], F32))

        loaded = [sem(f"loaded{s}") for s in range(SLOTS)]
        units_hi = sem("units_hi")
        units_split = sem("units_split")
        units_used = sem("units_used")
        rope_loaded = sem("rope_loaded")
        setup_loaded = sem("setup_loaded")
        final_gain_loaded = sem("final_gain_loaded")
        params1_loaded = sem("params1_loaded")
        params2_loaded = sem("params2_loaded")
        bias_loaded = sem("bias_loaded")
        x_stored = sem("x_stored")
        consts_ready = sem("consts_ready")
        gains_T = sem("gains_T")
        gains_ready = sem("gains_ready")
        gain_l_ready = sem("gain_l_ready")
        x_ready = sem("x_ready")
        squares = sem("squares")
        mean_sq = sem("mean_sq")
        roots = sem("roots")
        rstd_ready = sem("rstd_ready")
        xn_ready = sem("xn_ready")
        stage_T = sem("stage_T")
        stage_hi = sem("stage_hi")
        stage_ready = sem("stage_ready")
        silu_done = sem("silu_done")
        g_ready = sem("g_ready")
        g_T = sem("g_T")
        gT_hi_done = sem("gT_hi_done")
        gT_ready = sem("gT_ready")
        down_done = sem("down_done")
        up_half_done = sem("up_half_done")
        proj_act = sem("proj_act")
        proj_dve = sem("proj_dve")
        pos_T = sem("pos_T")
        pos_ready = sem("pos_ready")
        tj_done = sem("tj_done")
        tj_act = sem("tj_act")
        tj_dve = sem("tj_dve")
        rot_ready = sem("rot_ready")
        twice_ready = sem("twice_ready")
        flat_ready = sem("flat_ready")
        flat_hi_done = sem("flat_hi_done")
        flat_lo_done = sem("flat_lo_done")
        gelu_done = sem("gelu_done")
        h1_T = sem("h1_T")
        h1T_ready = sem("h1T_ready")
        kv_c = sem("kv_c")
        kv_c_ready = sem("kv_c_ready")
        cs_done = sem("cs_done")
        cs_shifted = sem("cs_shifted")
        c_exp = sem("c_exp")
        c_probs = sem("c_probs")
        c_T = sem("c_T")
        cT_ready = sem("cT_ready")
        c_out = sem("c_out")
        c_evac = sem("c_evac")
        gates_done = sem("gates_done")
        scores_done = sem("scores_done")
        scores_masked = sem("scores_masked")
        probs_ready = sem("probs_ready")
        probs_T = sem("probs_T")
        pT_ready = sem("pT_ready")
        attn_done = sem("attn_done")
        attn_evac = sem("attn_evac")
        rope_arg = sem("rope_arg")
        rope_sin = sem("rope_sin")
        lam_sums = sem("lam_sums")
        lam_exp = sem("lam_exp")
        tables_ready = sem("tables_ready")
        par_free = sem("par_free")
        head_sq = sem("head_sq")
        head_ms = sem("head_ms")
        head_root = sem("head_root")
        head_scale = sem("head_scale")
        idx_done = sem("idx_done")
        idx_relu = sem("idx_relu")
        idx_used = sem("idx_used")
        yb_sq = sem("yb_sq")
        yb_ms = sem("yb_ms")
        yb_root = sem("yb_root")
        yb_scale = sem("yb_scale")
        yb_ready = sem("yb_ready")
        gates2_ready = sem("gates2_ready")
        wait_over = sem("wait_over")

        def heads(ap, n):
            return ap.unsqueeze(ap.ndim - 1).broadcast_to(list(ap.shape[:-1]) + [n, ap.shape[-1]])

        def lanes(ap, n):
            return ap.unsqueeze(ap.ndim).broadcast_to(list(ap.shape) + [n])

        def job1(j):
            if j < 8:
                h = j
                return (DH * (h // 4), 4 + h % 4, 8, 896 + DH * (h // 4), DH, DH * h, 3 * h + 1, False)
            if j < 16:
                h = j - 8
                return (DH * (h // 4), 4 + h % 4, 9, 1152 + DH * (h // 4), DH, DH * h, 3 * h + 2, True)
            h = j - 16
            return (DH * (h % 2), 10 + h // 2, 14 + h // 2, 2328 + DH * h, DH, 512 + DH * h, None, False)

        def job2(j):
            if j < 8:
                h, c = j // 2, j % 2
                return (DH * c, 16 + h, 20 + h, 2884 + P * h, P, 512 + P * h, 1 if c else None, c == 1)
            h = j - 8
            return (DH * (h % 2), h // 2, 4 + h // 2, 1024 + DH * h, DH, DH * h, None, False)

        def items1(k, n=1):
            return tt1[:, k:k + n, :]

        def items2(k, n=1):
            if k < 16:
                return tt2[:, k:k + n, :]
            k -= 16
            return proj2[:, k // 4, 256 * (k % 4):256 * (k % 4) + 256 * n].rearrange("p (c n) -> p c n", c=n)

        def paired(ap):
            return ap.rearrange("p (r g d) -> p g r d", g=2, d=DH)

        TJOBS1 = [(0, 128), (256, 384), ("k0", "k1"), ("v0", "v1"), (0, 128), (256, 384), (768, 1024),
                  (1304, 1432), (1560, 1688), (1816, 1944), (2072, 2200)]
        ITEM1 = [0, 2, None, None, 4, 6, 8, 10, 12, 14, 16]
        TJOBS2 = [(0, 128), (256, 384), (512, 640), (768, 896), (1536, 1664), ("k", ),
                  (1860, 1988), (2116, 2244), (2372, 2500), (2628, 2756)]
        ITEM2 = [0, 2, 4, 6, 8, 10, 16, 18, 20, 22]
        NEGATED1, NEGATED2 = (6, 9, 10), (2, 3, 8, 9)

        PARTS = ((0, 0), (0, 1), (1, 0), (1, 1))
        BANK1 = (0, 2, 0, 2, 0, 0)
        BANK2 = (0, 2, 0, 2, 0, 2, 0, 0, 0, 0, 0)
        HEAD_NORMS = ((0, 0, 0), (1, 512, 16), (2, 1792, 64), (3, 1860, 32), (4, 2372, 48))
        relu = xn[:, :, 0:384]
        h1 = tt1[0:30, 4:6, :].rearrange("p a n -> p (a n)").rearrange("p (k n) -> p k n", k=2)
        flat_csc = tt1[:, 6, 0:240].rearrange("p (h n) -> p h n", n=NCMP)
        flat_cex = tt1[:, 7, 0:240].rearrange("p (h n) -> p h n", n=NCMP)
        csc = tt1[:, 6, 0:240].rearrange("p (i h n) -> p i h n", i=2, h=8)
        cex = tt1[:, 7, 0:240].rearrange("p (i h n) -> p i h n", i=2, h=8)
        c_gated = tt1[:, 8:10, :].rearrange("p a n -> p (a n)")

        block = ctx.enter_context(nc.Block())

        @block.sync
        def _(sp):
            def load(st, p, pieces, it=0):
                sp.wait_ge(units_split, st.freed(p, it))
                assert len(pieces) == 2
                for dst, src in pieces:
                    sp.dma_start(dst, src).then_inc(loaded[p % SLOTS], 16)

            def rows_of(w, l, r0, n, c0, m):
                return w[bass.ds(l, 1), r0:r0 + n * P, c0:c0 + m].rearrange("a (c p) m -> p (a c) m", p=P)

            def slot4(p):
                return raw[:, p % SLOTS, :].rearrange("p (c n) -> p c n", c=4)

            def slot2(p):
                return raw[:, p % SLOTS, :].rearrange("p (c n) -> p c n", c=2)

            def ffn_loads(st, l, p0, wg, up_off, wu, wd):
                def tile(t, pt, it=0):
                    for j in range(2):
                        p = pt + j
                        load(st, p, [
                            (slot4(p)[:, :, 256 * k:256 * k + 256],
                             w[bass.ds(l, 1), 512 * j:512 * j + 512, bass.ds(t * 256 + off, 256)]
                             .rearrange("a (c p) m -> p (a c) m", p=P))
                            for k, (w, off) in enumerate(((wg, 0), (wu, up_off)))], it)
                for t in range(3):
                    tile(t, p0 + 2 * t)
                with sp.Fori(0, 4) as it:
                    tile(it * 2 + 3, p0 + 6, it)
                    tile(it * 2 + 4, p0 + 8, it)
                for u in range(U_DOWN):
                    wide(st, l, p0 + U_UP + u, wd, 256 * u)

            def wide(st, l, p, w, r0):
                load(st, p, [(slot2(p)[:, c:c + 1, :], rows_of(w, l, r0 + P * c, 1, 0, DM)) for c in range(2)])

            def win_loads(st, l, p0, w, tiles):
                for n, (c0, m) in enumerate(tiles):
                    for j in range(2):
                        p = p0 + 2 * n + j
                        load(st, p, [(slot4(p)[:, 2 * h:2 * h + 2, 0:m],
                                      rows_of(w, l, 512 * j + 256 * h, 2, c0, m)) for h in range(2)])

            sp.dma_start(inv_f[:, :], I["inv_freq2"].broadcast_to([P, 32])).then_inc(rope_loaded, 16)
            sp.dma_start(pos_i[:, :], I["positions_2"].rearrange("a (i p) -> p (a i)", p=P),
                         allow_slow_non_contiguous=True).then_inc(rope_loaded, 16)
            for i in range(2):
                sp.dma_start(x[:, i, :], I["x"][0, P * i:P * i + P, :]).then_inc(setup_loaded, 16)
            at = 0
            for name in ("norm_ffn1", "norm_mix", "norm_ffn2", "attn_norm_2", "ffn_norm_2"):
                sp.dma_start(gain_rows[at:at + L * KC, :], I[name].rearrange("l (c p) -> (l c) p", p=P))\
                    .then_inc(setup_loaded, 16)
                at += L * KC
            sp.dma_start(rot1[:, :, :], I["rot1"].rearrange("(i p) n -> p i n", p=P)).then_inc(setup_loaded, 16)

            with sp.Fori(0, L) as l:
                st = stream1(l)
                ffn_loads(st, l, P1_FFN1, I["w_ffn1_gate"], 0, I["w_ffn1_up"], I["w_ffn1_down"])
                sp.wait_ge(c_evac, l * 2 + 1)
                sp.dma_start(pos_rows[0:16, :], I["pos_ck"][bass.ds(l, 1)].rearrange("a (c j) d -> (a c) (j d)", j=2))\
                    .then_inc(params1_loaded, 16)
                sp.dma_start(pos_rows[16:32, :], I["pos_cv"][bass.ds(l, 1)].rearrange("a (c j) d -> (a c) (j d)", j=2))\
                    .then_inc(params1_loaded, 16)
                for d in range(2):
                    sp.dma_start(w_k2[:, :, d, :], I["w_ck2"][bass.ds(l, 1)].rearrange("a (k p) d -> p (a k) d", p=P))\
                        .then_inc(params1_loaded, 16)
                sp.dma_start(w_v2[:, :, :], I["w_cv2"][bass.ds(l, 1)].rearrange("a (k p) d -> p (a k) d", p=P))\
                    .then_inc(params1_loaded, 16)
                win_loads(st, l, P1_WIN, I["w_in"], WIN1)
                for u in range(4):
                    p = P1_CK + u
                    load(st, p, [(slot4(p)[:, :, 256 * k:256 * k + 256], rows_of(w, l, 512 * u, 4, 0, 256))
                                 for k, w in enumerate((I["w_ck1"], I["w_cv1"]))])
                for u in range(U_OUT):
                    wide(st, l, P1_OUT + u, I["w_out"], 256 * u)
                ffn_loads(st, l, P1_FFN2, I["w_ffn2_gate"], 0, I["w_ffn2_up"], I["w_ffn2_down"])
            sp.dma_start(row_gain, I["norm_final"].rearrange("(a n) -> a n", a=1).broadcast_to([P, DM]))\
                .then_inc(final_gain_loaded, 16)

            with sp.Fori(0, L) as l:
                st = stream2(l)
                sp.wait_ge(c_evac, 2 * L + 1)
                sp.wait_ge(par_free, l + 1)
                at = 0
                for name, m in (("a_q_norm_2", 64), ("a_k_norm_2", 64), ("idx_k_norm_2", 64), ("b_q_norm_2", 64),
                                ("b_k_norm_2", 64), ("b_subln_2", 128), ("diff_lambda_2", 256), ("lam_init", 2)):
                    src = I[name][bass.ds(l, 1)]
                    if name == "diff_lambda_2":
                        src = src.rearrange("a b c -> a (b c)")
                    sp.dma_start(par2[:, at:at + m], src.broadcast_to([P, m])).then_inc(params2_loaded, 16)
                    at += m
                win_loads(st, l, P2_WIN, I["w_in_2"], WIN2[:2])
                sp.wait_ge(squares, l * 2 + 8)
                sp.dma_start(proj2[:, 1, GATES2:GATES2 + 2 * DM],
                             I["gate_bias_2"][bass.ds(l, 1)].broadcast_to([P, 2 * DM])).then_inc(bias_loaded, 16)
                win_loads(st, l, P2_WIN + 4, I["w_in_2"], WIN2[2:])
                for u in range(2):
                    wide(st, l, P2_UPA + u, I["w_up_a_2"], 256 * u)
                for u in range(2):
                    wide(st, l, P2_UPB + u, I["w_up_b_2"], 256 * u)
                for u in range(U_OUT):
                    wide(st, l, P2_OUT + u, I["w_out_2"], 256 * u)
                ffn_loads(st, l, P2_FFN, I["w_ffn_in_2"], DFF, I["w_ffn_in_2"], I["w_ffn_out_2"])

            for i in range(2):
                sp.wait_ge(x_ready, 2 * (7 + 2 * L) + i + 1)
                sp.dma_start(out[0, P * i:P * i + P, :], x[:, i, :]).then_inc(x_stored, 16)
            sp.wait_ge(x_stored, 32)

        @block.gpsimd
        def _(pool):
            def select(ap, pattern, base, fill, op):
                nc.gpsimd.drain()
                nc.gpsimd.affine_select(out=ap, in_=ap, compare_op=op, fill=fill, base=base, pattern=pattern,
                                        channel_multiplier=1)
            nc.gpsimd.memset(ident[:, :], 0.0)
            nc.gpsimd.memset(causal[:, :], 0.0)
            nc.gpsimd.memset(cmask[:, :, :], 0.0)
            nc.gpsimd.memset(cvalid[:, :, :], 1.0)
            select(ident[:, :], [[-1, P]], 0, 1.0, ALU.not_equal)
            select(causal[:, 0:P], [[-1, P]], 0, -NEG, ALU.is_ge)
            select(causal[:, 2 * P:3 * P], [[-1, P]], 0, -NEG, ALU.is_ge)
            select(cmask[:, :, :], [[P, 2], [-16, NCMP]], -31, NEG, ALU.is_ge)
            select(cvalid[:, :, :], [[P, 2], [-16, NCMP]], -31, 0.0, ALU.is_ge)
            nc.gpsimd.drain()
            pool.sem_inc(consts_ready, 1)

            with pool.Fori(0, L) as l:
                pool.wait_ge(proj_act, l * len(WIN1) + 2)
                pool.wait_ge(proj_dve, l * len(WIN1) + 2)
                pool.sem_inc(wait_over, 1)
                for i in range(2):
                    nc.gpsimd.tensor_copy(twice1[:, i], heads(proj1[:, i, 512:768].rearrange("p (k d) -> p k d", d=DH), 2))
                nc.gpsimd.drain()
                pool.sem_inc(twice_ready, 1)
                def rotate(c0, n):
                    a = proj1[:, :, c0:c0 + n * DH].rearrange("p i (h d) -> p i h d", d=DH)
                    x1, x2 = a[:, :, :, 0:8], a[:, :, :, 8:16]
                    cos, sin = heads(rot1[:, :, 0:8], n), heads(rot1[:, :, 8:16], n)
                    tmp = [row_rot[:, k, :, 0:n, :] for k in range(4)]
                    nc.gpsimd.tensor_tensor(tmp[0], x1, cos, ALU.mult)
                    nc.gpsimd.tensor_tensor(tmp[1], x2, sin, ALU.mult)
                    nc.gpsimd.tensor_tensor(tmp[2], x2, cos, ALU.mult)
                    nc.gpsimd.tensor_tensor(tmp[3], x1, sin, ALU.mult)
                    nc.gpsimd.drain()
                    nc.gpsimd.tensor_tensor(x1, tmp[0], tmp[1], ALU.subtract)
                    nc.gpsimd.tensor_tensor(x2, tmp[2], tmp[3], ALU.add)
                    nc.gpsimd.drain()
                pool.wait_ge(tj_done, l * TJ1 + 2)
                pool.wait_ge(proj_act, l * len(WIN1) + 3)
                pool.wait_ge(proj_dve, l * len(WIN1) + 3)
                for c0, n in ((0, 8), (768, 2), (1024, 2)):
                    rotate(c0, n)
                pool.sem_inc(rot_ready, 1)
                pool.wait_ge(proj_act, l * len(WIN1) + 5)
                pool.wait_ge(proj_dve, l * len(WIN1) + 5)
                for c0, n in ((1304, 8), (1816, 8)):
                    rotate(c0, n)
                pool.sem_inc(rot_ready, 1)

            with pool.Fori(0, L) as l:
                def rotate2(c0, n, tabs, scale=None):
                    a = proj2[:, :, c0:c0 + n * DH].rearrange("p i (h d) -> p i h d", d=DH)
                    x1, x2 = a[:, :, :, 0:32], a[:, :, :, 32:64]
                    t1, t2 = (att[:, 1024 + 512 * k:1024 + 512 * k + 64 * n].rearrange("p (i h d) -> p i h d", i=2, d=32)
                              for k in range(2))
                    nc.gpsimd.tensor_tensor(t1, x2, heads(tabs[1], n), ALU.mult)
                    nc.gpsimd.tensor_tensor(t2, x1, heads(tabs[3], n), ALU.mult)
                    nc.gpsimd.drain()
                    if scale is not None:
                        pool.wait_ge(head_sq, scale[1])
                    nc.gpsimd.tensor_tensor(x1, x1, heads(tabs[0], n), ALU.mult)
                    nc.gpsimd.tensor_tensor(x2, x2, heads(tabs[2], n), ALU.mult)
                    nc.gpsimd.drain()
                    nc.gpsimd.tensor_tensor(x1, x1, t1, ALU.subtract)
                    nc.gpsimd.tensor_tensor(x2, x2, t2, ALU.add)
                    nc.gpsimd.drain()
                    if scale is not None:
                        pool.wait_ge(head_scale, scale[1])
                        for i in range(2):
                            nc.gpsimd.tensor_tensor(a[:, i], a[:, i], lanes(scale[0][:, i, :], DH), ALU.mult)
                        nc.gpsimd.drain()

                for q, (n, c0, m0) in enumerate(HEAD_NORMS):
                    pool.wait_ge(proj_act, l * 7 + (12 + n + 1))
                    pool.wait_ge(proj_dve, l * 11 + (12 + n + 1))
                    if n == 2:
                        rotate2(1536, 4, [cs2[:, 0], cs2[:, 1], cs2[:, 0], cs2[:, 1]])
                    w = 1 if n == 2 else 8
                    rotate2(c0, w, [rg[:, q, k] for k in range(4)],
                            (ms[:, m0:m0 + 2 * w].rearrange("p (i h) -> p i h", i=2), l * 5 + q + 1))
                    if n == 2:
                        nc.gpsimd.tensor_copy(twice2, heads(proj2[:, :, 1792:1856], 2))
                        nc.gpsimd.drain()
                    pool.sem_inc(rot_ready, 1)
                yb = xn[:, :, 512:1024].rearrange("p i (h d) -> p i h d", d=P)
                pool.wait_ge(attn_evac, l * JOBS2 + (JOBS1 * L + 8))
                for i in range(2):
                    nc.gpsimd.tensor_tensor(proj2[:, i, 2884:3396], xn[:, i, 512:1024], xn[:, i, 512:1024], ALU.mult)
                nc.gpsimd.drain()
                pool.sem_inc(yb_sq, 1)
                for i in range(2):
                    nc.gpsimd.tensor_tensor(yb[:, i], yb[:, i], heads(par2[:, 320:448], 4), ALU.mult)
                nc.gpsimd.drain()
                pool.wait_ge(yb_scale, l + 1)
                for i in range(2):
                    nc.gpsimd.tensor_tensor(yb[:, i], yb[:, i], lanes(ms[:, 4 * i:4 * i + 4], P), ALU.mult)
                nc.gpsimd.drain()
                pool.sem_inc(yb_ready, 1)
                pool.sem_inc(par_free, 1)

        @block.scalar
        def _(act):
            def split(st, p, it=0, m=None, c=4):
                s = p % SLOTS
                act.wait_ge(loaded[s], st.loads(p, it))
                act.wait_ge(units_used, st.freed(p, it))
                src, dst = raw[:, s, :], w_hi[:, s, :]
                if m is not None:
                    src, dst = (a.rearrange("p (c n) -> p c n", c=c)[:, :, 0:m] for a in (src, dst))
                nc.scalar.activation(dst, src, ACT.Copy).then_inc(units_hi, 1)

            def norm(X):
                for i in range(2):
                    act.wait_ge(x_ready, X * 2 + (i + 1))
                    nc.scalar.activation(xn[:, i, :], x[:, i, :], ACT.Square, accum_out=ss[:, i:i + 1])
                nc.scalar.drain()
                act.sem_inc(squares, 1)

            def root(X):
                act.wait_ge(mean_sq, X + 1)
                nc.scalar.activation(rstd[:, :], ss[:, :], ACT.Sqrt).then_inc(roots, 1)
                act.wait_ge(rstd_ready, X + 1)

            def stage(S, gain=None, parts=PARTS, first=0):
                for n, (i, g) in enumerate(parts, first):
                    act.wait_ge(stage_T, S * 4 + (n + 1))
                    bank = ps[:, 4 + 2 * i + g, :].rearrange("p (c t) -> p c t", c=4)
                    tok = slice(P * i, P * i + P)
                    if gain is None:
                        o = nc.scalar.activation(aT_hi[:, 4 * g:4 * g + 4, tok], bank, ACT.Copy)
                    else:
                        for c in range(4):
                            o = nc.scalar.activation(aT_hi[:, 4 * g + c, tok], bank[:, c], ACT.Copy,
                                                     scale=gain_l[:, gain, 4 * g + c:4 * g + c + 1])
                    o.then_inc(stage_hi, 1)

            def ffn(st, F, X, p0, nxt):
                norm(X)

                def tile(t, pt, it=0, first=False):
                    for j in range(2):
                        split(st, pt + 2 + j, it)
                    if first:
                        root(X)
                    act.wait_ge(units_used, st.used(pt + 1, it))
                    b = pt // 2 - p0 // 2
                    for i in range(2):
                        o = nc.scalar.activation(sil[:, b % 2, i], ps[:, 2 * (b % 2) + i, 0:256], ACT.Silu,
                                                 scale=rstd[:, i:i + 1])
                    o.then_inc(silu_done, 1)
                    if not first:
                        keep(t - 1, b + 1)

                def keep(t, b):
                    act.wait_ge(g_T, F * FT + t + 1)
                    nc.scalar.activation(gT_hi[:, bass.ds(t * 2, 2), :],
                                         ps[:, 4 + b % 2, :].rearrange("p (c n) -> p c n", c=2), ACT.Copy)\
                        .then_inc(gT_hi_done, 1)
                for t in range(3):
                    tile(t, p0 + 2 * t, first=(t == 0))
                with act.Fori(0, 4) as it:
                    tile(it * 2 + 3, p0 + 6, it)
                    tile(it * 2 + 4, p0 + 8, it)
                keep(FT - 1, FT - 1)
                for u in range(U_DOWN - 2):
                    split(st, p0 + U_UP + 2 + u)
                for args in nxt:
                    split(st, *args)

            def tj(T, k, dst, sign=1.0):
                act.wait_ge(tj_done, T + k + 1)
                nc.scalar.activation(dst, ps[:, 4 + k % 4, 0:dst.shape[1] * SEQ]
                                     .rearrange("p (c n) -> p c n", n=SEQ), ACT.Copy, scale=sign).then_inc(tj_act, 1)

            def jobs(J, a, b, first=None, last=None):
                for j in range(a if first is None else first, b + 4 if last is None else last):
                    if a <= j - 2 < b:
                        k = j - 2
                        act.wait_ge(probs_T, J + k + 1)
                        if k >= a + 2:
                            act.wait_ge(attn_done, J + k - 1)
                        nc.scalar.activation(pT_sb[:, k % 2, :], ps[:, 6 + k % 2, 0:384], ACT.Copy)\
                            .then_inc(pT_ready, 1)
                    if j < b:
                        act.wait_ge(scores_masked, (J + j) * 2 + 2)
                        for i, (c, n) in enumerate(((0, P), (P, 2 * P))):
                            o = nc.scalar.activation(p_sb[:, j % 4, c:c + n], p_sb[:, j % 4, c:c + n], ACT.Exp,
                                                     bias=neg_max[:, j % 4, i:i + 1], scale=-1.0,
                                                     accum_out=sums[:, j % 4, i:i + 1])
                        nc.scalar.drain()
                        act.sem_inc(probs_ready, 1)

            for n in range(2):
                act.wait_ge(rope_arg, n + 1)
                nc.scalar.activation(cs2[:, n, :, :], att[:, 64 * n:64 * n + 64].rearrange("p (i f) -> p i f", i=2),
                                     ACT.Sin).then_inc(rope_sin, 1)

            with act.Fori(0, L) as l:
                st = stream1(l)
                split(st, 0)
                act.wait_ge(gain_l_ready, l + 1)
                stage(l * 4, 0)
                split(st, 1)
                ffn(st, l * 2, l * 3, P1_FFN1, [(P1_WIN, 0, 512), (P1_WIN + 1, 0, 512)])
                stage(l * 4 + 1, 1)
                norm(l * 3 + 1)
                T, J = l * TJ1, l * JOBS1

                def evac(n):
                    c0, m = WIN1[n]
                    act.wait_ge(units_used, st.used(P1_WIN + 2 * n + 1))
                    dst, src = proj1[:, 0, c0:c0 + m], ps[:, BANK1[n], 0:m]
                    if n == 0:
                        dst, src = paired(dst), src.rearrange("p (g r d) -> p g r d", g=2, d=DH)
                    nc.scalar.activation(dst, src, ACT.Copy, scale=rstd[:, 0:1]).then_inc(proj_act, 1)
                for n in range(4):
                    for j in range(2):
                        split(st, P1_WIN + 2 * n + 2 + j, 0, WIN1[n + 1][1])
                    if n == 0:
                        root(l * 3 + 1)
                    evac(n)
                    if n == 2:
                        nc.scalar.drain()
                        act.wait_ge(proj_dve, l * 6 + 3)
                        nc.scalar.activation(gates1[:, :, :], proj1[:, :, 1280:1304], ACT.Sigmoid)\
                            .then_inc(gates_done, 1)
                tj(T, 0, tt1[:, 0:2, :])
                for j in range(2):
                    split(st, P1_WIN + 10 + j)
                act.wait_ge(flat_ready, l + 1)
                for k, dst in enumerate((kflat_hi, vflat_hi)):
                    o = nc.scalar.activation(dst[:, 0:480], att[:, 992 + 480 * k:992 + 480 * k + 480], ACT.Copy)
                o.then_inc(flat_hi_done, 1)
                evac(4)
                for k in (4, 6):
                    tj(T, k, tt1[:, ITEM1[k]:ITEM1[k] + 2, :], -1.0 if k in NEGATED1 else 1.0)
                for u in range(6):
                    split(st, P1_CK + u)
                    jobs(J, 0, 16, first=3 * u, last=3 * u + 3)
                    if u == 1:
                        evac(5)
                jobs(J, 0, 16, first=18)
                for k in (8, 10):
                    tj(T, k, tt1[:, ITEM1[k]:ITEM1[k] + 2, :], -1.0 if k in NEGATED1 else 1.0)
                act.wait_ge(units_used, st.used(P1_CK + 3))
                act.wait_ge(scores_done, J + 16)
                nc.scalar.activation(h1, ps[0:30, 0:2, 0:256], ACT.Gelu_apprx_tanh).then_inc(gelu_done, 1)
                for j in range(12):
                    jobs(J, 16, 24, first=16 + j, last=17 + j)
                    if j == 2:
                        act.wait_ge(cs_shifted, l + 1)
                        nc.scalar.activation(cex, csc, ACT.Exp, scale=DH ** -0.5).then_inc(c_exp, 1)
                    if j in (4, 6):
                        i = (j - 4) // 2
                        act.wait_ge(c_T, l * 4 + 2 * i + 1)
                        if i == 1:
                            act.wait_ge(c_out, l * 2 + 1)
                        nc.scalar.activation(pcT[0:NCMP, 0:4, :], ps[0:NCMP, 0, :]
                                             .rearrange("p (h n) -> p h n", h=4), ACT.Copy).then_inc(cT_ready, 1)
                stage(l * 4 + 2)
                for p in range(2, 4):
                    split(st, P1_OUT + p)
                split(st, P1_FFN2)
                split(st, P1_FFN2 + 1)
                stage(l * 4 + 3, 2)
                ffn(st, l * 2 + 1, l * 3 + 2, P1_FFN2, [])
            norm(6)
            root(6)

            with act.Fori(0, L) as l:
                st = stream2(l)
                split(st, 0)
                act.wait_ge(gain_l_ready, l + L + 1)
                stage(l * 4 + 8, 0)
                split(st, 1)
                X, W, T, J = l * 2 + 7, l * 11 + 12, l * TJ2 + TJ1 * L, l * JOBS2 + JOBS1 * L
                norm(X)

                def win_split(n, j):
                    split(st, P2_WIN + 2 * n + j, 0, WIN2[n][1])

                def evac(n):
                    c0, m = WIN2[n]
                    act.wait_ge(units_used, st.used(P2_WIN + 2 * n + 1))
                    nc.scalar.activation(proj2[:, 0, c0:c0 + m], ps[:, BANK2[n], 0:m], ACT.Copy,
                                         scale=rstd[:, 0:1]).then_inc(proj_act, 1)

                def head_squares(q):
                    n, c0, m0 = HEAD_NORMS[q]
                    nc.scalar.drain()
                    act.wait_ge(proj_dve, W + (n + 1))
                    if n != 2:
                        nc.scalar.activation(att[:, 0:1024].rearrange("p (i n) -> p i n", i=2),
                                             proj2[:, :, c0:c0 + 512], ACT.Square).then_inc(head_sq, 1)
                    else:
                        for i in range(2):
                            nc.scalar.activation(att[:, 64 * i:64 * i + 64], proj2[:, i, c0:c0 + DH], ACT.Square,
                                                 accum_out=ms[:, m0 + i:m0 + i + 1])
                        nc.scalar.drain()
                        act.sem_inc(head_sq, 1)

                def head_roots(q):
                    n, c0, m0 = HEAD_NORMS[q]
                    v = ms[:, m0:m0 + (2 if n == 2 else 16)]
                    act.wait_ge(head_ms, l * 5 + q + 1)
                    nc.scalar.activation(v, v, ACT.Sqrt).then_inc(head_root, 1)

                def item(k):
                    tj(T, k, items2(ITEM2[k], len(TJOBS2[k])), -1.0 if k in NEGATED2 else 1.0)

                def index_relu(h):
                    act.wait_ge(idx_done, l * 4 + h + 1)
                    if h >= 2:
                        act.wait_ge(idx_used, l * 4 + h - 1)
                    nc.scalar.activation(relu[:, h % 2, :], ps[:, 4 + h % 2, 0:384], ACT.Relu, scale=DH ** -0.5)\
                        .then_inc(idx_relu, 1)

                win_split(1, 0)
                win_split(1, 1)
                root(X)
                evac(0)
                head_squares(0)
                act.wait_ge(lam_sums, l + 1)
                nc.scalar.activation(lam[:, 0:2], lam[:, 0:2], ACT.Exp).then_inc(lam_exp, 1)
                for n in range(1, 4):
                    win_split(n + 1, 0)
                    head_roots(n - 1)
                    win_split(n + 1, 1)
                    evac(n)
                    head_squares(n)
                item(0)
                item(2)
                win_split(5, 0)
                head_roots(3)
                item(4)
                win_split(5, 1)
                index_relu(0)
                index_relu(1)
                evac(4)
                head_squares(4)
                win_split(6, 0)
                head_roots(4)
                index_relu(2)
                index_relu(3)
                win_split(6, 1)
                item(6)
                evac(5)
                win_split(7, 0)
                item(8)
                for u, n in enumerate(STEPS2):
                    p, j = JOBS2_FROM + u, sum(STEPS2[:u])
                    split(st, P2_WIN + p + 2)
                    jobs(J, 0, 16, first=j, last=j + n - 1)
                    if p == 13:
                        evac(6)
                    jobs(J, 0, 16, first=j + n - 1, last=j + n)
                act.wait_ge(yb_ms, l + 1)
                nc.scalar.activation(ms[:, 0:8], ms[:, 0:8], ACT.Sqrt).then_inc(yb_root, 1)
                stage(l * 4 + 9, parts=((0, 0), (1, 0)))
                split(st, P2_UPB)
                stage(l * 4 + 9, parts=((0, 1), (1, 1)), first=2)
                split(st, P2_UPB + 1)
                act.wait_ge(proj_dve, W + 11)
                for c0 in (GATES2, GATES2 + DM):
                    nc.scalar.activation(proj2[:, :, c0:c0 + DM], proj2[:, :, c0:c0 + DM], ACT.Sigmoid)\
                        .then_inc(gates2_ready, 1)
                for p in range(2):
                    split(st, P2_OUT + p)
                stage(l * 4 + 10)
                for p in range(2, 4):
                    split(st, P2_OUT + p)
                split(st, P2_FFN)
                split(st, P2_FFN + 1)
                stage(l * 4 + 11, 1)
                ffn(st, l + 4, l * 2 + 8, P2_FFN, [])

        @block.vector
        def _(dve):
            V = nc.vector

            def split(st, p, it=0, m=None, c=4):
                s = p % SLOTS
                dve.wait_ge(units_hi, st.index(p, it) + 1)
                a, h, o = raw[:, s, :], w_hi[:, s, :].bitcast(F32), w_lo[:, s, :]
                if m is not None:
                    a, h, o = (v.rearrange("p (c n) -> p c n", c=c)[:, :, 0:m] for v in (a, h, o))
                V.tensor_tensor(o, a, h, ALU.subtract).then_inc(units_split, 1)

            def norm(X):
                dve.wait_ge(squares, X + 1)
                V.tensor_scalar(ss[:, :], ss[:, :], 1.0 / DM, EPS, ALU.mult, ALU.add).then_inc(mean_sq, 1)
                dve.wait_ge(roots, X + 1)
                V.reciprocal(rstd[:, :], rstd[:, :]).then_inc(rstd_ready, 1)
                V.drain()

            def stage(S, gain=None, parts=PARTS, first=0):
                for n, (i, g) in enumerate(parts, first):
                    dve.wait_ge(stage_hi, S * 4 + (n + 1))
                    bank = ps[:, 4 + 2 * i + g, :].rearrange("p (c t) -> p c t", c=4)
                    tok = slice(P * i, P * i + P)
                    hi = aT_hi[:, 4 * g:4 * g + 4, tok].bitcast(F32)
                    if gain is None:
                        o = V.tensor_tensor(aT_lo[:, 4 * g:4 * g + 4, tok], bank, hi, ALU.subtract)
                    else:
                        for c in range(4):
                            o = V.scalar_tensor_tensor(aT_lo[:, 4 * g + c, tok], bank[:, c],
                                                       gain_l[:, gain, 4 * g + c:4 * g + c + 1], hi[:, c],
                                                       ALU.mult, ALU.subtract)
                    o.then_inc(stage_ready, 1)

            def residual(st, R, p_last, scale, S=None, gain=None):
                for i in range(2):
                    if i == 0:
                        dve.wait_ge(down_done, R + 1)
                    else:
                        dve.wait_ge(units_used, st.used(p_last))
                    for n in range(2):
                        xs = x[:, i, 512 * n:512 * n + 512]
                        o = V.scalar_tensor_tensor(xs, ps[:, 2 * i + n, :], scale, xs, ALU.mult, ALU.add)
                    o.then_inc(x_ready, 1)
                    if i == 0 and S is not None:
                        stage(S, gain, PARTS[:1])

            def ffn(st, F, R, X, p0, nxt, scale=0.5, S=None, gain=None):
                def tile(t, pt, it=0, first=False):
                    for j in range(2):
                        split(st, pt + 2 + j, it)
                    if first:
                        norm(X)
                    b = pt // 2 - p0 // 2
                    dve.wait_ge(silu_done, F * FT + t + 1)
                    for i in range(2):
                        o = V.scalar_tensor_tensor(gg[:, b % 2, i], ps[:, 2 * (b % 2) + i, 256:512],
                                                   rstd[:, i:i + 1], sil[:, b % 2, i], ALU.mult, ALU.mult)
                    o.then_inc(g_ready, 1)
                    if not first:
                        keep(t - 1, b + 1)

                def keep(t, b):
                    dve.wait_ge(gT_hi_done, F * FT + t + 1)
                    V.tensor_tensor(gT_lo[:, bass.ds(t * 2, 2), :],
                                    ps[:, 4 + b % 2, :].rearrange("p (c n) -> p c n", c=2),
                                    gT_hi[:, bass.ds(t * 2, 2), :].bitcast(F32), ALU.subtract).then_inc(gT_ready, 1)
                for t in range(3):
                    tile(t, p0 + 2 * t, first=(t == 0))
                with dve.Fori(0, 4) as it:
                    tile(it * 2 + 3, p0 + 6, it)
                    tile(it * 2 + 4, p0 + 8, it)
                keep(FT - 1, FT - 1)
                for u in range(U_DOWN - 2):
                    split(st, p0 + U_UP + 2 + u)
                for args in nxt:
                    split(st, *args)
                residual(st, R, p0 + U_UP + U_DOWN - 1, scale, S, gain)

            def tj(T, k, dst, sign=1.0):
                dve.wait_ge(tj_done, T + k + 1)
                V.tensor_scalar(dst, ps[:, 4 + k % 4, 0:dst.shape[1] * SEQ].rearrange("p (c n) -> p c n", n=SEQ),
                                sign, None, ALU.mult).then_inc(tj_dve, 1)

            def jobs(J, a, b, job, mask, block2=False, first=None, last=None):
                for j in range(a if first is None else first, b + 4 if last is None else last):
                    V.drain()
                    if j < b:
                        dve.wait_ge(scores_done, J + j + 1)
                        if j >= a + 4:
                            dve.wait_ge(probs_T, J + j - 3)
                        dve.sem_inc(wait_over, 1)
                        for i, (c, n) in enumerate(((0, P), (P, 2 * P))):
                            V.tensor_tensor_reduce(out=p_sb[:, j % 4, c:c + n], in0=ps[:, 4 + j % 2, c:c + n],
                                                   in1=mask(j)[:, c:c + n], scale=DH ** -0.5, scalar=3.0e38,
                                                   op0=ALU.add, op1=ALU.min, accum_out=neg_max[:, j % 4, i:i + 1])\
                                .then_inc(scores_masked, 1)
                    if a <= j - 2 < b:
                        dve.wait_ge(probs_ready, J + j - 1)
                        V.reciprocal(factor[:, (j - 2) % 4, :], sums[:, (j - 2) % 4, :])
                    if a <= j - 3 < b:
                        gate = job(j - 3)[6]
                        f = factor[:, (j - 3) % 4, :]
                        if not block2 and gate is not None:
                            V.tensor_tensor(f, f, gates1[:, :, gate], ALU.mult)
                        if block2 and gate is not None:
                            V.tensor_scalar(f, f, lam[:, 2:3], None, ALU.mult)
                    if j >= a + 4:
                        k = j - 4
                        _, _, _, _, m, o0, _, add = job(k)
                        dve.wait_ge(attn_done, J + k + 1)
                        for i in range(2):
                            o = xn[:, i, o0:o0 + m]
                            src = ps[:, 2 + k % 2, P * i:P * i + m]
                            f = factor[:, k % 4, i:i + 1]
                            if add:
                                q = V.scalar_tensor_tensor(o, src, f, o, ALU.mult, ALU.add)
                            else:
                                q = V.tensor_scalar(o, src, f, None, ALU.mult)
                        q.then_inc(attn_evac, 1)
                V.drain()

            dve.sem_inc(units_split, SLOTS)
            dve.sem_inc(par_free, 1)
            dve.sem_inc(c_evac, 1)
            C1 = 6.28125
            C2 = float(np.float32(np.round((2 * math.pi - C1) * 2.0 ** 19) / 2.0 ** 19))
            C3 = float(np.float32(2 * math.pi - C1 - C2))
            MAGIC = 12582912.0
            dve.wait_ge(rope_loaded, 32)
            V.tensor_copy(pos_f[:, :], pos_i[:, :])
            V.drain()
            ang = att[:, 128:192].rearrange("p (i f) -> p i f", i=2)
            turns = att[:, 192:256]
            for i in range(2):
                V.tensor_scalar(ang[:, i, :], inv_f[:, :], pos_f[:, i:i + 1], None, ALU.mult)
            V.drain()
            for n, (turn, shift) in enumerate(((0.25, math.pi / 2), (0.0, 0.0))):
                r = att[:, 64 * n:64 * n + 64]
                V.tensor_scalar(turns, att[:, 128:192], 1.0 / (2 * math.pi), turn, ALU.mult, ALU.add)
                V.drain()
                V.tensor_scalar(turns, turns, MAGIC, None, ALU.add)
                V.drain()
                V.tensor_scalar(turns, turns, MAGIC, None, ALU.subtract)
                V.drain()
                V.scalar_tensor_tensor(r, turns, -C1, att[:, 128:192], ALU.mult, ALU.add)
                V.drain()
                V.scalar_tensor_tensor(r, turns, -C2, r, ALU.mult, ALU.add)
                V.drain()
                V.scalar_tensor_tensor(r, turns, -C3, r, ALU.mult, ALU.add)
                V.drain()
                V.tensor_scalar(r, r, shift, 3.1415925, ALU.add, ALU.min)
                V.drain()
                V.tensor_scalar(r, r, -3.1415925, None, ALU.max).then_inc(rope_arg, 1)
            dve.wait_ge(rope_sin, 2)
            dve.wait_ge(setup_loaded, 16 * 8)
            dve.wait_ge(gains_T, 1)
            V.tensor_copy(gain_cols[:, :], ps[:, 0, 0:80]).then_inc(gains_ready, 1)
            V.drain()
            dve.sem_inc(x_ready, 2)

            with dve.Fori(0, L) as l:
                st = stream1(l)
                for k in range(3):
                    V.tensor_copy(gain_l[:, k, :], gain_cols[:, bass.ds(l * KC + 16 * k, KC)])
                V.drain()
                dve.sem_inc(gain_l_ready, 1)
                split(st, 0)
                stage(l * 4, 0)
                split(st, 1)
                ffn(st, l * 2, l * 3, l * 3, P1_FFN1, [(P1_WIN, 0, 512), (P1_WIN + 1, 0, 512)],
                    S=l * 4 + 1, gain=1)
                stage(l * 4 + 1, 1, PARTS[1:], first=1)
                for t in (kflat_hi, kflat_lo, vflat_hi, vflat_lo):
                    V.memset(t[:, 480:578].bitcast(F32), 0.0)
                T, J = l * TJ1, l * JOBS1

                def evac(n):
                    c0, m = WIN1[n]
                    dve.wait_ge(units_used, st.used(P1_WIN + 2 * n + 1))
                    dst, src = proj1[:, 1, c0:c0 + m], ps[:, BANK1[n] + 1, 0:m]
                    if n == 0:
                        dst, src = paired(dst), src.rearrange("p (g r d) -> p g r d", g=2, d=DH)
                    V.tensor_scalar(dst, src, rstd[:, 1:2], None, ALU.mult).then_inc(proj_dve, 1)
                for n in range(4):
                    for j in range(2):
                        split(st, P1_WIN + 2 * n + 2 + j, 0, WIN1[n + 1][1])
                    if n == 0:
                        norm(l * 3 + 1)
                        dve.wait_ge(pos_T, l + 1)
                        V.tensor_copy(posT[:, :], ps[:, 3, 0:32]).then_inc(pos_ready, 1)
                        V.drain()
                    evac(n)
                tj(T, 1, tt1[:, 2:4, :])
                for k in range(2):
                    dve.wait_ge(tj_done, T + 2 + k + 1)
                    src = ps[:, 6 + k, :].rearrange("p (g t) -> p g t", g=2)
                    for g in range(2):
                        for j in range(2):
                            q = slice(DH * j, DH * j + DH)
                            for half in range(2):
                                tok = src[q, g, 16 * half:16 * half + 240].rearrange("p (n c) -> p c n", c=16)
                                tok = tok[:, j::2, :]
                                pos = posT[q, 16 * k + 8 * half:16 * k + 8 * half + 8]
                                o = V.tensor_tensor(flat[q, k, 8 * half:8 * half + 8, g, :], tok, lanes(pos, NCMP),
                                                    ALU.add)
                    o.then_inc(tj_dve, 1)
                V.drain()
                dve.sem_inc(flat_ready, 1)
                for j in range(2):
                    split(st, P1_WIN + 10 + j)
                dve.wait_ge(flat_hi_done, l + 1)
                for k, (h, lo) in enumerate(((kflat_hi, kflat_lo), (vflat_hi, vflat_lo))):
                    o = V.tensor_tensor(lo[:, 0:480], att[:, 992 + 480 * k:992 + 480 * k + 480],
                                        h[:, 0:480].bitcast(F32), ALU.subtract)
                o.then_inc(flat_lo_done, 1)
                evac(4)
                tj(T, 5, tt1[:, 6:8, :])
                dve.wait_ge(gates_done, l + 1)
                dve.sem_inc(wait_over, 1)
                for u in range(6):
                    jobs(J, 0, 16, job1, lambda j: causal, first=3 * u, last=3 * u + 1)
                    split(st, P1_CK + u)
                    jobs(J, 0, 16, job1, lambda j: causal, first=3 * u + 1, last=3 * u + 3)
                    if u == 1:
                        evac(5)
                jobs(J, 0, 16, job1, lambda j: causal, first=18)
                for k in (7, 9):
                    tj(T, k, tt1[:, ITEM1[k]:ITEM1[k] + 2, :], -1.0 if k in NEGATED1 else 1.0)
                for j in range(12):
                    jobs(J, 16, 24, job1, lambda j: causal, first=16 + j, last=17 + j)
                    if j == 0:
                        dve.wait_ge(h1_T, l + 1)
                        V.tensor_copy(h1T[:, :, :], ps[:, 0, 0:128].rearrange("p (k n) -> p k n", k=4)[:, :, 0:30])\
                            .then_inc(h1T_ready, 1)
                    if j == 1:
                        dve.wait_ge(kv_c, l + 1)
                        V.tensor_copy(kcT[:, :], ps[:, 1, 0:30])
                        V.tensor_copy(vc[0:NCMP, :, :], ps[0:NCMP, 1, 64:192].rearrange("p (g d) -> p g d", g=2))\
                            .then_inc(kv_c_ready, 1)
                    if j == 2:
                        dve.wait_ge(cs_done, l + 1)
                        for i in range(2):
                            for g in range(2):
                                V.tensor_tensor(csc[:, i, 4 * g:4 * g + 4],
                                                ps[:, g, 64 * i:64 * i + 64]
                                                .rearrange("p (h n) -> p h n", h=4)[:, :, 0:NCMP],
                                                heads(cmask[:, i, :], 4), ALU.add)
                        V.drain()
                        V.tensor_reduce(cmp_max[:, :], flat_csc, AX.X, ALU.max)
                        V.drain()
                        V.tensor_tensor(flat_csc, flat_csc, lanes(cmp_max[:, :], NCMP), ALU.subtract)\
                            .then_inc(cs_shifted, 1)
                    if j == 3:
                        dve.wait_ge(c_exp, l + 1)
                        for i in range(2):
                            V.tensor_tensor(cex[:, i], cex[:, i], heads(cvalid[:, i, :], 8), ALU.mult)
                        V.drain()
                        V.tensor_reduce(cmp_max[:, :], flat_cex, AX.X, ALU.add)
                        V.drain()
                        V.tensor_scalar(cmp_max[:, :], cmp_max[:, :], 1.0, None, ALU.max)
                        V.drain()
                        V.reciprocal(cmp_max[:, :], cmp_max[:, :])
                        V.drain()
                        V.tensor_tensor(flat_cex, flat_cex, lanes(cmp_max[:, :], NCMP), ALU.mult).then_inc(c_probs, 1)
                    if j in (4, 6):
                        i = (j - 4) // 2
                        dve.wait_ge(c_T, l * 4 + 2 * i + 2)
                        V.tensor_copy(pcT[0:NCMP, 4:8, :], ps[0:NCMP, 1, :].rearrange("p (h n) -> p h n", h=4))\
                            .then_inc(cT_ready, 1)
                    if j in (5, 7):
                        i = (j - 5) // 2
                        dve.wait_ge(c_out, l * 2 + i + 1)
                        V.tensor_tensor(c_gated.rearrange("p (h d) -> p h d", d=DH),
                                        ps[:, 0, :].rearrange("p (h d) -> p h d", d=DH),
                                        lanes(gates1[:, i, 0:24:3], DH), ALU.mult)
                        V.drain()
                        V.tensor_tensor(xn[:, i, 0:512], xn[:, i, 0:512], c_gated, ALU.add).then_inc(c_evac, 1)
                dve.sem_inc(xn_ready, 2)
                stage(l * 4 + 2)
                for p in range(2, 4):
                    split(st, P1_OUT + p)
                split(st, P1_FFN2)
                split(st, P1_FFN2 + 1)
                residual(st, l * 3 + 1, P1_OUT + U_OUT - 1, 1.0, S=l * 4 + 3, gain=2)
                stage(l * 4 + 3, 2, PARTS[1:], first=1)
                ffn(st, l * 2 + 1, l * 3 + 2, l * 3 + 2, P1_FFN2, [])
            norm(6)
            dve.wait_ge(final_gain_loaded, 16)
            for i in range(2):
                V.scalar_tensor_tensor(x[:, i, :], x[:, i, :], rstd[:, i:i + 1], row_gain, ALU.mult, ALU.mult)\
                    .then_inc(x_ready, 1)

            with dve.Fori(0, L) as l:
                st = stream2(l)
                for k in range(2):
                    V.tensor_copy(gain_l[:, k, :], gain_cols[:, bass.ds(l * KC + 48 + 16 * k, KC)])
                V.drain()
                dve.sem_inc(gain_l_ready, 1)
                split(st, 0)
                stage(l * 4 + 8, 0)
                split(st, 1)
                dve.wait_ge(params2_loaded, (l + 1) * 128)
                for n in range(5):
                    g = par2[:, 64 * n:64 * n + 64]
                    for k, (trig, half) in enumerate(((0, 0), (1, 1), (0, 1), (1, 0))):
                        V.tensor_tensor(rg[:, n, k], cs2[:, trig],
                                        heads(g[:, 32 * half:32 * half + 32], 2), ALU.mult)
                dl = par2[:, 448:704].rearrange("p (a b d) -> p a b d", a=2, b=2)
                V.tensor_tensor(score[:, 0:128].rearrange("p (a d) -> p a d", a=2), dl[:, :, 0, :], dl[:, :, 1, :],
                                ALU.mult)
                V.drain()
                V.tensor_reduce(lam[:, 0:2], score[:, 0:128].rearrange("p (a d) -> p a d", a=2), AX.X, ALU.add)\
                    .then_inc(lam_sums, 1)
                V.tensor_scalar(par2[:, 320:448], par2[:, 320:448], par2[:, 705:706], None, ALU.mult)
                X, W, T, J = l * 2 + 7, l * 11 + 12, l * TJ2 + TJ1 * L, l * JOBS2 + JOBS1 * L

                def win_split(n, j):
                    split(st, P2_WIN + 2 * n + j, 0, WIN2[n][1])

                def evac(n):
                    c0, m = WIN2[n]
                    dve.wait_ge(units_used, st.used(P2_WIN + 2 * n + 1))
                    if c0 < GATES2:
                        V.tensor_scalar(proj2[:, 1, c0:c0 + m], ps[:, BANK2[n] + 1, 0:m], rstd[:, 1:2], None,
                                        ALU.mult).then_inc(proj_dve, 1)
                        return
                    if n == 7:
                        dve.wait_ge(bias_loaded, (l + 1) * 16)
                    for i in range(2):
                        V.scalar_tensor_tensor(proj2[:, i, c0:c0 + m], ps[:, BANK2[n] + i, :], rstd[:, i:i + 1],
                                               proj2[:, 1, c0:c0 + m], ALU.mult, ALU.add)
                        V.drain()
                    dve.sem_inc(proj_dve, 1)

                def head_sums(q):
                    n, c0, m0 = HEAD_NORMS[q]
                    v = ms[:, m0:m0 + (2 if n == 2 else 16)]
                    dve.wait_ge(head_sq, l * 5 + q + 1)
                    if n != 2:
                        V.tensor_reduce(v, att[:, 0:1024].rearrange("p (h d) -> p h d", d=DH), AX.X, ALU.add)
                        V.drain()
                    V.tensor_scalar(v, v, 1.0 / DH, EPS, ALU.mult, ALU.add).then_inc(head_ms, 1)

                def head_scales(q):
                    n, c0, m0 = HEAD_NORMS[q]
                    v = ms[:, m0:m0 + (2 if n == 2 else 16)]
                    dve.wait_ge(head_root, l * 5 + q + 1)
                    V.reciprocal(v, v).then_inc(head_scale, 1)

                def item(k):
                    tj(T, k, items2(ITEM2[k], len(TJOBS2[k])), -1.0 if k in NEGATED2 else 1.0)

                def index_score(h):
                    dve.wait_ge(idx_relu, l * 4 + h + 1)
                    for i, (c, n) in enumerate(((0, P), (P, 2 * P))):
                        V.scalar_tensor_tensor(score[:, c:c + n], relu[:, h % 2, c:c + n], iw[:, i, h:h + 1],
                                               (causal if h == 0 else score)[:, c:c + n], ALU.mult,
                                               ALU.subtract if h == 0 else ALU.add)
                    V.drain()
                    dve.sem_inc(idx_used, 1)

                def best(rounds):
                    for _ in range(rounds):
                        for i, (c, n) in enumerate(((0, P), (P, 2 * P))):
                            V.max(m8[:, i, :], score[:, c:c + n])
                        V.drain()
                        for i, (c, n) in enumerate(((0, P), (P, 2 * P))):
                            V.match_replace(score[:, c:c + n], m8[:, i, :], score[:, c:c + n], TAKEN)
                        V.drain()

                win_split(1, 0)
                win_split(1, 1)
                norm(X)
                evac(0)
                head_sums(0)
                dve.wait_ge(lam_exp, l + 1)
                V.tensor_tensor(lam[:, 2:3], lam[:, 1:2], lam[:, 0:1], ALU.subtract)
                V.drain()
                V.tensor_tensor(lam[:, 2:3], lam[:, 2:3], par2[:, 704:705], ALU.subtract)
                for n in range(1, 4):
                    win_split(n + 1, 0)
                    head_scales(n - 1)
                    win_split(n + 1, 1)
                    evac(n)
                    head_sums(n)
                    if n == 2:
                        V.tensor_scalar(iw[:, :, :], proj2[:, :, 1856:1860], 0.5, None, ALU.mult)
                item(1)
                item(3)
                win_split(5, 0)
                head_scales(3)
                item(5)
                win_split(5, 1)
                index_score(0)
                index_score(1)
                evac(4)
                head_sums(4)
                win_split(6, 0)
                head_scales(4)
                index_score(2)
                index_score(3)
                win_split(6, 1)
                item(7)
                best(1)
                evac(5)
                win_split(7, 0)
                best(1)
                item(9)
                best(1)
                for u, n in enumerate(STEPS2):
                    p, j = JOBS2_FROM + u, sum(STEPS2[:u])
                    mask2 = lambda k: causal if k < 8 else score
                    jobs(J, 0, 16, job2, mask2, True, first=j, last=j + 1)
                    split(st, P2_WIN + p + 2)
                    jobs(J, 0, 16, job2, mask2, True, first=j + 1, last=j + n - 1)
                    if p % 2 == 1 and p < 21:
                        evac(p // 2)
                    jobs(J, 0, 16, job2, mask2, True, first=j + n - 1, last=j + n)
                    if p < 17:
                        best(2 if p == 15 else 1)
                    if p == 16:
                        V.tensor_scalar(score[:, :], score[:, :], TAKEN, -NEG, ALU.not_equal, ALU.mult)
                        V.drain()
                        V.tensor_tensor(score[:, :], score[:, :], causal[:, :], ALU.add)
                        V.drain()
                    if p == 19:
                        dve.wait_ge(yb_sq, l + 1)
                        V.tensor_reduce(ms[:, 0:8].rearrange("p (i h) -> p i h", i=2),
                                        proj2[:, :, 2884:3396].rearrange("p i (h d) -> p i h d", d=P), AX.X, ALU.add)
                        V.drain()
                        V.tensor_scalar(ms[:, 0:8], ms[:, 0:8], 1.0 / P, EPS, ALU.mult, ALU.add).then_inc(yb_ms, 1)
                dve.sem_inc(xn_ready, 2)
                evac(10)
                stage(l * 4 + 9, parts=((0, 0), (1, 0)))
                dve.wait_ge(yb_root, l + 1)
                V.reciprocal(ms[:, 0:8], ms[:, 0:8]).then_inc(yb_scale, 1)
                split(st, P2_UPB)
                stage(l * 4 + 9, parts=((0, 1), (1, 1)), first=2)
                split(st, P2_UPB + 1)
                dve.wait_ge(units_used, st.used(P2_UPA + 1))
                dve.wait_ge(gates2_ready, l * 2 + 1)
                for i in range(2):
                    V.tensor_tensor(xn[:, i, :].rearrange("p (n c) -> p n c", n=2), ps[:, 2 * i:2 * i + 2, :],
                                    proj2[:, i, GATES2:GATES2 + DM].rearrange("p (n c) -> p n c", n=2), ALU.mult)
                for p in range(2):
                    split(st, P2_OUT + p)
                dve.wait_ge(gates2_ready, l * 2 + 2)
                for i in range(2):
                    if i == 0:
                        dve.wait_ge(up_half_done, l + 1)
                    else:
                        dve.wait_ge(units_used, st.used(P2_UPB + 1))
                    gb = proj2[:, i, GATES2 + DM:GATES2 + 2 * DM]
                    V.tensor_tensor(gb.rearrange("p (n c) -> p n c", n=2), ps[:, 4 + 2 * i:6 + 2 * i, :],
                                    gb.rearrange("p (n c) -> p n c", n=2), ALU.mult)
                    V.drain()
                    V.tensor_tensor(xn[:, i, :], xn[:, i, :], gb, ALU.add).then_inc(xn_ready, 1)
                    if i == 0:
                        stage(l * 4 + 10, parts=PARTS[:1])
                stage(l * 4 + 10, parts=PARTS[1:], first=1)
                for p in range(2, 4):
                    split(st, P2_OUT + p)
                split(st, P2_FFN)
                split(st, P2_FFN + 1)
                residual(st, l * 2 + 6, P2_OUT + U_OUT - 1, 1.0, S=l * 4 + 11, gain=1)
                stage(l * 4 + 11, 1, PARTS[1:], first=1)
                ffn(st, l + 4, l * 2 + 7, l * 2 + 8, P2_FFN, [], scale=1.0)

        @block.tensor
        def _(pe):
            M = nc.tensor.matmul

            def three(o, ah, al, wh, wl, start, stop):
                M(o, ah, wh, start=start, stop=False)
                M(o, ah, wl, start=False, stop=False)
                return M(o, al, wh, start=False, stop=stop)

            def split_ready(st, p, it=0):
                pe.wait_ge(units_split, st.index(p, it) + (1 + SLOTS))

            def turned(src, i, g):
                for c in range(4):
                    o = nc.tensor.transpose(ps[:, 4 + 2 * i + g, P * c:P * c + P],
                                            src[:, i, P * (4 * g + c):P * (4 * g + c) + P], ident[:, :])
                o.then_inc(stage_T, 1)

            def stage(src, ready, n, i):
                pe.wait_ge(ready, n * 2 + (i + 1))
                turned(src, i, 0)
                turned(src, i, 1)

            def second_half(src, ready, n):
                return lambda j, k: stage(src, ready, n, 1) if (j, k) == (0, 1) else None

            def full_k(st, S, pt, it, bank, m, beside=None):
                for j in range(2):
                    p = pt + j
                    split_ready(st, p, it)
                    for i in range(2):
                        if S is not None:
                            pe.wait_ge(stage_ready, S * 4 + (4 if j == 1 else 1 + 2 * i))
                        for c in range(4):
                            k = 4 * j + c
                            o = three(ps[:, bank + i, 0:m], aT_hi[:, k, P * i:P * i + P], aT_lo[:, k, P * i:P * i + P],
                                      w_hi[:, p % SLOTS, 512 * c:512 * c + m], w_lo[:, p % SLOTS, 512 * c:512 * c + m],
                                      k == 0, k == KC - 1)
                            if i == 1 and c == 3:
                                o.then_inc(units_used, 1)
                            if beside is not None:
                                beside(j, 4 * i + c)

            def wide(st, p, u, last, src_hi, src_lo, k0, bank=0, done=None, order=(0, 1),
                     between=None, late=None):
                split_ready(st, p)
                for i in order:
                    if between is not None and i == order[1]:
                        between()
                    for n in range(2):
                        for c in range(2):
                            if late is not None and (i, n, c) == (order[1], 1, 0):
                                late()
                            k = k0 + c
                            w = 1024 * c + 512 * n
                            o = three(ps[:, bank + 2 * i + n, :], src_hi[:, k, P * i:P * i + P],
                                      src_lo[:, k, P * i:P * i + P], w_hi[:, p % SLOTS, w:w + 512],
                                      w_lo[:, p % SLOTS, w:w + 512], u == 0 and c == 0, last and c == 1)
                    if last and done is not None and i == 0:
                        o.then_inc(done, 1)
                return o

            def ffn(st, F, S, p0, X, nxt=None):
                def tile(t, pt, it=0, stat=None):
                    b = pt // 2 - p0 // 2
                    if stat is None or stat >= 2:
                        pe.wait_ge(g_ready, F * FT + t - 1)
                    full_k(st, S if stat == 0 else None, pt, it, 2 * (b % 2), 512,
                           second_half(x, x_ready, X) if stat == 0 else None)

                def turn(t, b, stat=None):
                    pe.wait_ge(g_ready, F * FT + t + 1)
                    if stat is None or stat >= 2:
                        pe.wait_ge(gT_ready, F * FT + t - 1)
                    for c in range(2):
                        for i in range(2):
                            o = nc.tensor.transpose(ps[:, 4 + b % 2, SEQ * c + P * i:SEQ * c + P * i + P],
                                                    gg[:, b % 2, i, P * c:P * c + P], ident[:, :])
                    o.then_inc(g_T, 1)

                def both(t, pt, it=0, stat=None):
                    tile(t, pt, it, stat)
                    b = pt // 2 - p0 // 2
                    if stat is None or stat >= 1:
                        turn(t - 1, b + 1, None if stat is None else stat - 1)
                for t in range(3):
                    both(t, p0 + 2 * t, 0, t)
                with pe.Fori(0, 4) as it:
                    both(it * 2 + 3, p0 + 6, it)
                    both(it * 2 + 4, p0 + 8, it)
                for u in range(U_DOWN):
                    pe.wait_ge(gT_ready, F * FT + u + 1)
                    o = wide(st, p0 + U_UP + u, u, u == U_DOWN - 1, gT_hi, gT_lo, 2 * u, done=down_done,
                             order=(1, 0) if u == 0 else (0, 1),
                             between=(lambda: turn(FT - 1, FT - 1)) if u == 0 else None,
                             late=(lambda: stage(x, x_ready, nxt, 0)) if u == U_DOWN - 1 and nxt is not None else None)
                    o.then_inc(units_used, 1)

            def out_proj(st, S, p0, nx, X):
                def second():
                    stage(xn, xn_ready, nx, 1)
                    pe.wait_ge(stage_ready, S * 4 + 3)
                for u in range(U_OUT):
                    if u in (0, 1):
                        pe.wait_ge(stage_ready, S * 4 + (1 if u == 0 else 4))
                    o = wide(st, p0 + u, u, u == U_OUT - 1, aT_hi, aT_lo, 2 * u, done=down_done,
                             between=second if u == 0 else None,
                             late=(lambda: stage(x, x_ready, X, 0)) if u == U_OUT - 1 else None)
                    o.then_inc(units_used, 1)

            def tjobs(T, ks, jobs, src, kfree):
                for k in ks:
                    kfree(k)
                    for e, c0 in enumerate(jobs[k]):
                        for i in range(2):
                            if c0 == "k":
                                block_in = twice2[:, i].rearrange("p e d -> p (e d)")
                            elif isinstance(c0, str):
                                block_in = twice1[:, i, 2 * (k - 2) + e].rearrange("p e d -> p (e d)")
                            else:
                                block_in = src[:, i, c0:c0 + P]
                            o = nc.tensor.transpose(ps[:, 4 + k % 4, SEQ * e + P * i:SEQ * e + P * i + P],
                                                    block_in, ident[:, :])
                    o.then_inc(tj_done, 1)

            def scores(qT, kT, q0, bank):
                q = slice(q0, q0 + DH)
                M(ps[:, bank, 0:P], qT[q, 0:P], kT[q, 0:P], start=True, stop=True)
                return M(ps[:, bank, P:3 * P], qT[q, P:2 * P], kT[q, :], start=True, stop=True)

            def jobs(J, a, b, job, items, src, first=None, last=None):
                for j in range(a if first is None else first, b + 4 if last is None else last):
                    if a <= j - 2 < b:
                        k = j - 2
                        pe.wait_ge(probs_ready, J + k + 1)
                        if k >= a + 2:
                            pe.wait_ge(pT_ready, J + k - 1)
                        for s in range(3):
                            o = nc.tensor.transpose(ps[:, 6 + k % 2, P * s:P * s + P], p_sb[:, k % 4, P * s:P * s + P],
                                                    ident[:, :])
                        o.then_inc(probs_T, 1)
                    if j < b:
                        q0, qi, ki = job(j)[:3]
                        if j >= a + 2:
                            pe.wait_ge(scores_masked, (J + j) * 2 - 2)
                        scores(items(qi)[:, 0], items(ki)[:, 0], q0, 4 + j % 2).then_inc(scores_done, 1)
                    if a <= j - 3 < b:
                        k = j - 3
                        v0, m = job(k)[3:5]
                        pe.wait_ge(pT_ready, J + k + 1)
                        if k >= a + 2:
                            pe.wait_ge(attn_evac, J + k - 1)
                        M(ps[:, 2 + k % 2, 0:m], pT_sb[:, k % 2, 0:P], src[:, 0, v0:v0 + m], start=True, stop=True)
                        M(ps[:, 2 + k % 2, P:P + m], pT_sb[:, k % 2, P:2 * P], src[:, 0, v0:v0 + m],
                          start=True, stop=False)
                        M(ps[:, 2 + k % 2, P:P + m], pT_sb[:, k % 2, 2 * P:3 * P], src[:, 1, v0:v0 + m],
                          start=False, stop=True).then_inc(attn_done, 1)

            pe.sem_inc(units_used, SLOTS)
            pe.wait_ge(consts_ready, 1)
            pe.wait_ge(setup_loaded, 16 * 8)
            nc.tensor.transpose(ps[:, 0, 0:80], gain_rows[:, :], ident[0:80, 0:80]).then_inc(gains_T, 1)

            with pe.Fori(0, L) as l:
                st = stream1(l)
                stage(x, x_ready, l * 3, 0)
                ffn(st, l * 2, l * 4, P1_FFN1, l * 3, l * 3 + 1)
                T, J = l * TJ1, l * JOBS1

                def tile(n, beside=None):
                    if n == 1:
                        pe.wait_ge(pos_ready, l + 1)
                    if n >= 2:
                        free = n if n == 5 else n - 1
                        pe.wait_ge(proj_act, l * 6 + free)
                        pe.wait_ge(proj_dve, l * 6 + free)
                    full_k(st, l * 4 + 1 if n == 0 else None, P1_WIN + 2 * n, 0, BANK1[n], WIN1[n][1], beside)
                def beside0(j, k):
                    if (j, k) == (0, 1):
                        stage(x, x_ready, l * 3 + 1, 1)
                        pe.wait_ge(params1_loaded, (l + 1) * 80)
                        pe.sem_inc(wait_over, 1)
                        nc.tensor.transpose(ps[:, 3, 0:32], pos_rows[:, :], ident[0:32, 0:32]).then_inc(pos_T, 1)
                for n in range(4):
                    tile(n, beside0 if n == 0 else None)
                pe.wait_ge(twice_ready, l + 1)
                tjobs(T, range(4), TJOBS1, proj1, lambda k: None)
                tile(4)
                pe.wait_ge(rot_ready, l * 2 + 1)

                def free1(k):
                    if k == 4:
                        pe.wait_ge(tj_act, l * 5 + 1)
                    else:
                        pe.wait_ge(tj_dve, l * 6 + (k - 4))
                tjobs(T, range(4, 7), TJOBS1, proj1, free1)
                pe.wait_ge(tj_act, l * 5 + 3)
                pe.wait_ge(tj_dve, l * 6 + 4)
                pe.wait_ge(proj_act, l * 6 + 4)
                pe.wait_ge(proj_dve, l * 6 + 4)

                def nsa(u, n):
                    if n in (2, 5, 7):
                        j = 3 * u + (2, 5, 7).index(n)
                        jobs(J, 0, 16, job1, items1, proj1, first=j, last=j + 1)
                tile(5, nsa)
                pe.wait_ge(flat_lo_done, l + 1)
                pe.wait_ge(proj_act, l * 6 + 6)
                pe.wait_ge(proj_dve, l * 6 + 6)
                for u in range(4):
                    p = P1_CK + u
                    split_ready(st, p)
                    for c in range(4):
                        k = 4 * u + c
                        for n, (h, lo) in enumerate(((kflat_hi, kflat_lo), (vflat_hi, vflat_lo))):
                            w = 512 * c + 256 * n
                            o = three(ps[:, n, 0:256], h[:, 30 * k:30 * k + P], lo[:, 30 * k:30 * k + P],
                                      w_hi[:, p % SLOTS, w:w + 256], w_lo[:, p % SLOTS, w:w + 256],
                                      k == 0, k == 15)
                            if c == 3 and n == 1:
                                o.then_inc(units_used, 1)
                            nsa(2 + u, 2 * c + n)
                jobs(J, 0, 16, job1, items1, proj1, first=18)
                pe.wait_ge(rot_ready, l * 2 + 2)
                tjobs(T, range(7, 11), TJOBS1, proj1, lambda k: None)
                pe.wait_ge(tj_act, l * 5 + 5)
                pe.wait_ge(tj_dve, l * 6 + 6)
                for j in range(12):
                    jobs(J, 16, 24, job1, items1, proj1, first=16 + j, last=17 + j)
                    if j == 0:
                        pe.wait_ge(gelu_done, l + 1)
                        pe.sem_inc(wait_over, 1)
                        for n in range(2):
                            for k in range(2):
                                o = nc.tensor.transpose(ps[:, 0, 32 * (2 * n + k):32 * (2 * n + k) + 30],
                                                        h1[:, n, P * k:P * k + P], ident[0:30, 0:30])
                        o.then_inc(h1_T, 1)
                    if j == 1:
                        pe.wait_ge(h1T_ready, l + 1)
                        for k in range(2):
                            M(ps[:, 1, 0:30], w_k2[:, k, :, :].rearrange("p a d -> p (a d)"), h1T[:, k, :],
                              start=k == 0, stop=k == 1)
                        for g in range(2):
                            for k in range(2):
                                o = M(ps[0:NCMP, 1, 64 + DH * g:64 + DH * g + DH],
                                      h1T[:, 2 + k, NCMP * g:NCMP * g + NCMP], w_v2[:, k, :],
                                      start=k == 0, stop=k == 1)
                        o.then_inc(kv_c, 1)
                    if j == 2:
                        pe.wait_ge(kv_c_ready, l + 1)
                        for i in range(2):
                            for h in range(8):
                                g = h // 4
                                q = slice(DH * g, DH * g + DH)
                                at = 64 * i + 16 * (h % 4)
                                o = M(ps[:, g, at:at + NCMP], tt1[q, h % 4, P * i:P * i + P],
                                      kcT[q, NCMP * g:NCMP * g + NCMP], start=True, stop=True)
                        o.then_inc(cs_done, 1)
                    if j in (4, 6):
                        i = (j - 4) // 2
                        pe.wait_ge(c_probs, l + 1)
                        if i == 1:
                            pe.wait_ge(c_evac, l * 2 + 2)
                        for half in range(2):
                            for h in range(4):
                                o = nc.tensor.transpose(ps[0:NCMP, half, P * h:P * h + P],
                                                        cex[:, i, 4 * half + h, :], ident[:, :])
                            o.then_inc(c_T, 1)
                    if j in (5, 7):
                        i = (j - 5) // 2
                        pe.wait_ge(cT_ready, l * 4 + 2 * i + 2)
                        for h in range(8):
                            o = M(ps[:, 0, DH * h:DH * h + DH], pcT[0:NCMP, h, :], vc[0:NCMP, h // 4, :],
                                  start=True, stop=True)
                        o.then_inc(c_out, 1)
                stage(xn, xn_ready, l, 0)
                out_proj(st, l * 4 + 2, P1_OUT, l, l * 3 + 2)
                ffn(st, l * 2 + 1, l * 4 + 3, P1_FFN2, l * 3 + 2)

            with pe.Fori(0, L) as l:
                st = stream2(l)
                stage(x, x_ready, l * 2 + 7, 0)
                T, J, W, A, D = l * TJ2 + TJ1 * L, l * JOBS2 + JOBS1 * L, l * 11 + 12, l * 5 + 10, l * 5 + 12

                def tile2(n, beside=None):
                    if n >= 2:
                        free = n if n >= 7 else n - 1
                        if n < 8:
                            pe.wait_ge(proj_act, l * 7 + (12 + free))
                        pe.wait_ge(proj_dve, W + free)
                    full_k(st, l * 4 + 8 if n == 0 else None, P2_WIN + 2 * n, 0, BANK2[n], WIN2[n][1], beside)

                def index_scores(h):
                    scores(tt2[:, 8 + h // 2, :], tt2[:, 10, :], DH * (h % 2), 4 + h % 2).then_inc(idx_done, 1)

                def beside4(j, n):
                    if (j, n) == (0, 3):
                        pe.wait_ge(rot_ready, l * 5 + (2 * L + 3))
                        pe.wait_ge(tj_act, A + 1)
                        pe.wait_ge(tj_dve, D + 1)
                        tjobs(T, range(4, 6), TJOBS2, proj2, lambda k: None)
                    if (j, n) == (1, 3):
                        pe.wait_ge(tj_act, A + 3)
                        pe.wait_ge(tj_dve, D + 3)
                        index_scores(0)
                        index_scores(1)

                def beside5(j, n):
                    if (j, n) == (0, 3):
                        pe.wait_ge(idx_relu, l * 4 + 1)
                        index_scores(2)
                        pe.wait_ge(idx_relu, l * 4 + 2)
                        index_scores(3)
                    if (j, n) == (1, 3):
                        pe.wait_ge(rot_ready, l * 5 + (2 * L + 4))
                        pe.wait_ge(tj_act, A + 2)
                        pe.wait_ge(tj_dve, D + 2)
                        tjobs(T, range(6, 8), TJOBS2, proj2, lambda k: None)

                def steps(j, n, t):
                    u = 2 * t + j - JOBS2_FROM
                    if u >= 0 and n in STEP_AT[STEPS2[u]]:
                        k = sum(STEPS2[:u]) + STEP_AT[STEPS2[u]].index(n)
                        jobs(J, 0, 16, job2, items2, proj2, first=k, last=k + 1)

                def beside6(j, n):
                    if (j, n) == (0, 3):
                        pe.wait_ge(rot_ready, l * 5 + (2 * L + 5))
                        pe.wait_ge(idx_relu, l * 4 + 4)
                        tjobs(T, range(8, 10), TJOBS2, proj2, lambda k: None)
                    if (j, n) == (1, 0):
                        pe.wait_ge(tj_act, A + 5)
                        pe.wait_ge(tj_dve, D + 5)
                        pe.wait_ge(proj_act, l * 7 + (12 + 6))
                        pe.wait_ge(proj_dve, W + 6)
                    steps(j, n, 6)

                for n in range(4):
                    tile2(n, second_half(x, x_ready, l * 2 + 7) if n == 0 else None)
                pe.wait_ge(rot_ready, l * 5 + (2 * L + 2))
                tjobs(T, range(4), TJOBS2, proj2, lambda k: None)
                tile2(4, beside4)
                tile2(5, beside5)
                tile2(6, beside6)
                for n in range(7, 11):
                    tile2(n, lambda j, k: steps(j, k, n))
                pe.wait_ge(xn_ready, (l * 2 + 2) * 2 + 2)
                turned(xn, 0, 0)
                turned(xn, 1, 0)
                pe.wait_ge(proj_dve, W + 11)
                pe.wait_ge(stage_ready, (l * 4 + 9) * 4 + 2)
                for u in range(2):
                    wide(st, P2_UPA + u, u, u == 1, aT_hi, aT_lo, 2 * u).then_inc(units_used, 1)
                    if u == 0:
                        pe.wait_ge(yb_ready, l + 1)
                        turned(xn, 0, 1)
                        turned(xn, 1, 1)
                pe.wait_ge(stage_ready, (l * 4 + 9) * 4 + 4)
                for u in range(2):
                    wide(st, P2_UPB + u, u, u == 1, aT_hi, aT_lo, 4 + 2 * u, bank=4, done=up_half_done,
                         late=(lambda: stage(xn, xn_ready, l * 2 + 3, 0)) if u == 1 else None).then_inc(units_used, 1)
                out_proj(st, l * 4 + 10, P2_OUT, l * 2 + 3, l * 2 + 8)
                ffn(st, l + 4, l * 4 + 11, P2_FFN, l * 2 + 8)


_INS = ["x", "norm_ffn1", "w_ffn1_gate", "w_ffn1_up", "w_ffn1_down", "norm_mix", "w_in", "pos_ck", "w_ck1", "w_ck2",
        "pos_cv", "w_cv1", "w_cv2", "w_out", "norm_ffn2", "w_ffn2_gate", "w_ffn2_up", "w_ffn2_down", "norm_final",
        "positions_2", "attn_norm_2", "w_in_2", "gate_bias_2", "a_q_norm_2", "a_k_norm_2", "idx_k_norm_2",
        "b_q_norm_2", "b_k_norm_2", "diff_lambda_2", "b_subln_2", "w_up_a_2", "w_up_b_2", "w_out_2", "ffn_norm_2",
        "w_ffn_in_2", "w_ffn_out_2"]


def shape_constants():
    f = np.float32
    inv1 = np.power(f(500000.0), -(np.arange(0, 16, 2, dtype=f) / f(16))).astype(f)
    ang = np.arange(SEQ, dtype=f)[:, None] * inv1[None, :]
    inv2 = (f(1.0) / np.power(f(10000.0), np.arange(0, DH, 2, dtype=f) / f(DH))).astype(f)
    init = [0.8 - 0.6 * math.exp(-0.3 * l) for l in range(DEPTH)]
    return {"rot1": np.concatenate([np.cos(ang), np.sin(ang)], axis=1).astype(f),
            "inv_freq2": inv2[None, :],
            "lam_init": np.array([[v, 1.0 - v] for v in init], dtype=f)}


def kernel(**inputs):
    import concourse.bacc as _bacc
    from concourse.bass_utils import run_bass_kernel_spmd as _run

    nc = _bacc.Bacc("TRN2", target_bir_lowering=False, num_devices=1)
    arrays, aps = {}, {}
    given = {name: np.ascontiguousarray(inputs[name]) for name in _INS}
    given.update(shape_constants())
    for name, a in given.items():
        arrays[f"in_{name}"] = a
        aps[name] = nc.dram_tensor(f"in_{name}", a.shape, mybir.dt.from_np(a.dtype), kind="ExternalInput").ap()
    out = nc.dram_tensor("out_x", (1, SEQ, DM), F32, kind="ExternalOutput").ap()
    build(nc, aps, out)
    return _run(nc, [arrays], core_ids=[0]).results[0]["out_x"]
```
